# Optimizing a Trainium2 kernel written in Bass

```python
import math
import jax, jax.numpy as jnp
from jax import lax
import numpy as np
import jax
import jax.numpy as jnp

D_MODEL = 2048
BATCH = 1
SEQ = 256
DEPTH = 1

NUM_MIXERS = 2
N_GLA_LAYERS = (DEPTH + NUM_MIXERS - 1) // NUM_MIXERS
N_GDN_LAYERS = DEPTH // NUM_MIXERS

EPS = 1e-6
CHUNK = 64
PLE_DIM = 256
D_FF = ((8 * D_MODEL + 3 * 256 - 1) // (3 * 256)) * 256

GLA_HEADS = 4
GLA_DK = D_MODEL // (2 * GLA_HEADS)
GLA_DV = D_MODEL // GLA_HEADS
GLA_KEY_DIM = GLA_HEADS * GLA_DK
GLA_VAL_DIM = GLA_HEADS * GLA_DV
GLA_GATE_RANK = 16
GLA_GATE_NORM = 16.0
GLA_PROJ = 2 * GLA_KEY_DIM + 2 * GLA_VAL_DIM + 2 * GLA_GATE_RANK

GDN_QK_HEADS = D_MODEL // 128
GDN_V_HEADS = 2 * GDN_QK_HEADS
GDN_DK = 128
GDN_DV = 128
GDN_KEY_DIM = GDN_QK_HEADS * GDN_DK
GDN_VAL_DIM = GDN_V_HEADS * GDN_DV
GDN_CONV_DIM = 2 * GDN_KEY_DIM + GDN_VAL_DIM
CONV_W = 5
GDN_PROJ = GDN_CONV_DIM + GDN_VAL_DIM + 4 * GDN_V_HEADS


def rmsnorm(x, w):
    xf = x.astype(jnp.float32)
    y = xf * lax.rsqrt(jnp.mean(xf * xf, axis=-1, keepdims=True) + EPS)
    return (y * w.astype(jnp.float32)).astype(x.dtype)

def l2norm(x):
    xf = x.astype(jnp.float32)
    return xf * lax.rsqrt(jnp.sum(xf * xf, axis=-1, keepdims=True) + EPS)

def to_heads(x, n):
    b, t, _ = x.shape
    return x.reshape(b, t, n, -1).transpose(0, 2, 1, 3)

def from_heads(x):
    b, n, t, d = x.shape
    return x.transpose(0, 2, 1, 3).reshape(b, t, n * d)

def flip_t(x):
    return jnp.flip(x, axis=2)

def gla_chunked(q, k, v, g):
    b, h, t, dk = q.shape
    dv = v.shape[-1]
    nc = t // CHUNK
    q, k, g = (a.reshape(b, h, nc, CHUNK, dk) for a in (q, k, g))
    v = v.reshape(b, h, nc, CHUNK, dv)
    cum = jnp.cumsum(g, axis=-2)
    last = cum[..., -1:, :]
    q_dec = q * jnp.exp(cum)
    k_dec = k * jnp.exp(last - cum)
    chunk_decay = jnp.exp(last[..., 0, :])
    lower = jnp.tril(jnp.ones((CHUNK, CHUNK), dtype=bool))
    xs = tuple(jnp.moveaxis(a, 2, 0) for a in (q, k, v, cum, q_dec, k_dec, chunk_decay))

    def step(S, inp):
        q_i, k_i, v_i, c_i, qd_i, kd_i, cd_i = inp
        pair = jnp.where(lower[..., None],
                         jnp.exp(jnp.minimum(c_i[..., :, None, :] - c_i[..., None, :, :], 0.0)), 0.0)
        a_i = jnp.einsum('bhid,bhjd,bhijd->bhij', q_i, k_i, pair)
        o_i = jnp.einsum('bhij,bhjv->bhiv', a_i, v_i) + jnp.einsum('bhid,bhdv->bhiv', qd_i, S)
        S = S * cd_i[..., None] + jnp.einsum('bhcd,bhcv->bhdv', kd_i, v_i)
        return S, o_i

    S0 = jnp.zeros((b, h, dk, dv), jnp.float32)
    _, o = lax.scan(step, S0, xs)
    return jnp.moveaxis(o, 0, 2).reshape(b, h, t, dv)

def gated_delta_chunked(q, k, v, g, beta):
    b, h, t, dk = q.shape
    dv = v.shape[-1]
    nc = t // CHUNK
    q = q.reshape(b, h, nc, CHUNK, dk)
    k = k.reshape(b, h, nc, CHUNK, dk)
    v = v.reshape(b, h, nc, CHUNK, dv)
    cum = jnp.cumsum(g.reshape(b, h, nc, CHUNK), axis=-1)
    beta = beta.reshape(b, h, nc, CHUNK, 1)
    idx = jnp.arange(CHUNK)
    lower = idx[:, None] >= idx[None, :]
    strict = idx[:, None] > idx[None, :]
    decay = jnp.where(lower, jnp.exp(jnp.minimum(cum[..., :, None] - cum[..., None, :], 0.0)), 0.0)
    k_beta = k * beta
    tri = jnp.where(strict, jnp.einsum('bhnid,bhnjd->bhnij', k_beta, k) * decay, 0.0) \
        + jnp.eye(CHUNK, dtype=jnp.float32)
    rhs = jnp.concatenate([v * beta, k_beta * jnp.exp(cum)[..., None]], axis=-1)
    sol = lax.linalg.triangular_solve(tri, rhs, left_side=True, lower=True, unit_diagonal=True)
    u, w = sol[..., :dv], sol[..., dv:]
    attn = jnp.einsum('bhnid,bhnjd->bhnij', q, k) * decay
    last = cum[..., -1:]
    q_dec = q * jnp.exp(cum)[..., None]
    k_dec = k * jnp.exp(last - cum)[..., None]
    chunk_decay = jnp.exp(last)
    xs = tuple(jnp.moveaxis(a, 2, 0) for a in (u, w, attn, q_dec, k_dec, chunk_decay))

    def step(S, inp):
        u_i, w_i, a_i, qd_i, kd_i, cd_i = inp
        v_new = u_i - jnp.einsum('bhcd,bhdv->bhcv', w_i, S)
        o_i = jnp.einsum('bhcd,bhdv->bhcv', qd_i, S) + jnp.einsum('bhij,bhjv->bhiv', a_i, v_new)
        S = S * cd_i[..., None] + jnp.einsum('bhcd,bhcv->bhdv', kd_i, v_new)
        return S, o_i

    S0 = jnp.zeros((b, h, dk, dv), jnp.float32)
    _, o = lax.scan(step, S0, xs)
    return jnp.moveaxis(o, 0, 2).reshape(b, h, t, dv)

def centred_short_conv(x, w):
    c = x.shape[-1]
    return lax.conv_general_dilated(
        x, w[:, None, :].astype(x.dtype), window_strides=(1,),
        padding=[(CONV_W // 2, CONV_W // 2)],
        dimension_numbers=('NWC', 'WIO', 'NWC'), feature_group_count=c)

def gla_mixer(hn, w_in, w_gate_up, b_gate, out_norm, w_out):
    b, t, _ = hn.shape
    proj = jnp.einsum('btd,de->bte', hn, w_in)
    q, k, v, og, lr = jnp.split(
        proj, [GLA_KEY_DIM, 2 * GLA_KEY_DIM, 2 * GLA_KEY_DIM + GLA_VAL_DIM,
               2 * GLA_KEY_DIM + 2 * GLA_VAL_DIM], axis=-1)
    lr = lr.reshape(b, t, 2, GLA_GATE_RANK)
    gk = jnp.einsum('btzr,zrd->zbtd', lr, w_gate_up) + b_gate[:, None, None, :]
    logdec = jax.nn.log_sigmoid(gk.astype(jnp.float32)) / GLA_GATE_NORM
    qh = to_heads(q, GLA_HEADS).astype(jnp.float32) * (GLA_DK ** -0.5)
    kh = to_heads(k, GLA_HEADS).astype(jnp.float32)
    vh = to_heads(v, GLA_HEADS).astype(jnp.float32)
    g_fwd = to_heads(logdec[0], GLA_HEADS)
    g_bwd = to_heads(logdec[1], GLA_HEADS)
    o = gla_chunked(qh, kh, vh, g_fwd) \
        + flip_t(gla_chunked(flip_t(qh), flip_t(kh), flip_t(vh), flip_t(g_bwd)))
    o = rmsnorm(o, out_norm)
    o = from_heads(o).astype(hn.dtype) * jax.nn.silu(og)
    return jnp.einsum('bte,ed->btd', o, w_out)

def gdn_mixer(hn, w_in, conv_w, a_log, dt_bias, out_norm, w_out):
    b, t, _ = hn.shape
    proj = jnp.einsum('btd,de->bte', hn, w_in)
    qkv, z, ba = jnp.split(proj, [GDN_CONV_DIM, GDN_CONV_DIM + GDN_VAL_DIM], axis=-1)
    qkv = jax.nn.silu(centred_short_conv(qkv, conv_w))
    q, k, v = jnp.split(qkv, [GDN_KEY_DIM, 2 * GDN_KEY_DIM], axis=-1)
    rep = GDN_V_HEADS // GDN_QK_HEADS
    qh = jnp.repeat(l2norm(to_heads(q, GDN_QK_HEADS)), rep, axis=1) * (GDN_DK ** -0.5)
    kh = jnp.repeat(l2norm(to_heads(k, GDN_QK_HEADS)), rep, axis=1)
    vh = to_heads(v, GDN_V_HEADS).astype(jnp.float32)
    ba = ba.reshape(b, t, 2, 2, GDN_V_HEADS).astype(jnp.float32)
    beta = jax.nn.sigmoid(ba[:, :, 0]).transpose(2, 0, 3, 1)
    a_in = ba[:, :, 1].transpose(2, 0, 3, 1)
    g = -jnp.exp(a_log.astype(jnp.float32))[:, None, :, None] \
        * jax.nn.softplus(a_in + dt_bias.astype(jnp.float32)[:, None, :, None])
    o = gated_delta_chunked(qh, kh, vh, g[0], beta[0]) \
        + flip_t(gated_delta_chunked(flip_t(qh), flip_t(kh), flip_t(vh), flip_t(g[1]), flip_t(beta[1])))
    o = rmsnorm(o, out_norm)
    o = from_heads(o).astype(hn.dtype) * jax.nn.silu(z)
    return jnp.einsum('bte,ed->btd', o, w_out)

def swiglu(hn, w_in, w_out):
    gate, up = jnp.split(jnp.einsum('btd,de->bte', hn, w_in), 2, axis=-1)
    return jnp.einsum('btf,fd->btd', jax.nn.silu(gate) * up, w_out)

def first_inputs(seed: int = 0) -> dict:
    key = jax.random.key(seed)
    ks = jax.random.split(key, 21)
    f32 = jnp.float32

    def nrm(k, shape, scale):
        return jax.random.normal(k, shape, f32) * scale

    def gain(k, shape):
        return 1.0 + 0.05 * jax.random.normal(k, shape, f32)

    x = nrm(ks[0], (BATCH, SEQ, D_MODEL), 1.0)
    p = nrm(ks[1], (DEPTH, BATCH, SEQ, PLE_DIM), 1.0)
    mixer_norm = gain(ks[2], (DEPTH, D_MODEL))
    gla_w_in = nrm(ks[3], (N_GLA_LAYERS, D_MODEL, GLA_PROJ), D_MODEL ** -0.5)
    gla_w_gate_up = nrm(ks[4], (N_GLA_LAYERS, 2, GLA_GATE_RANK, GLA_KEY_DIM), GLA_GATE_RANK ** -0.5)
    gla_b_gate = nrm(ks[5], (N_GLA_LAYERS, 2, GLA_KEY_DIM), 0.5)
    gla_out_norm = gain(ks[6], (N_GLA_LAYERS, GLA_DV))
    gla_w_out = nrm(ks[7], (N_GLA_LAYERS, GLA_VAL_DIM, D_MODEL), GLA_VAL_DIM ** -0.5)
    gdn_w_in = nrm(ks[8], (N_GDN_LAYERS, D_MODEL, GDN_PROJ), D_MODEL ** -0.5)
    gdn_conv = nrm(ks[9], (N_GDN_LAYERS, CONV_W, GDN_CONV_DIM), CONV_W ** -0.5)
    gdn_a_log = jnp.log(jax.random.uniform(ks[10], (N_GDN_LAYERS, 2, GDN_V_HEADS), f32, 1.0, 16.0))
    dt = jnp.exp(jax.random.uniform(ks[11], (N_GDN_LAYERS, 2, GDN_V_HEADS), f32,
                                    math.log(1e-3), math.log(1e-1)))
    gdn_dt_bias = dt + jnp.log(-jnp.expm1(-dt))
    gdn_out_norm = gain(ks[12], (N_GDN_LAYERS, GDN_DV))
    gdn_w_out = nrm(ks[13], (N_GDN_LAYERS, GDN_VAL_DIM, D_MODEL), GDN_VAL_DIM ** -0.5)
    ffn_norm = gain(ks[14], (DEPTH, D_MODEL))
    ffn_w_in = nrm(ks[15], (DEPTH, D_MODEL, 2 * D_FF), D_MODEL ** -0.5)
    ffn_w_out = nrm(ks[16], (DEPTH, D_FF, D_MODEL), D_FF ** -0.5)
    ple_norm = gain(ks[17], (DEPTH, D_MODEL))
    ple_w_gate = nrm(ks[18], (DEPTH, D_MODEL, D_MODEL), D_MODEL ** -0.5)
    ple_w_proj = nrm(ks[19], (DEPTH, PLE_DIM, D_MODEL), PLE_DIM ** -0.5)
    final_norm = gain(ks[20], (D_MODEL,))
    return {"x": x, "p": p, "mixer_norm": mixer_norm,
            "gla_w_in": gla_w_in, "gla_w_gate_up": gla_w_gate_up, "gla_b_gate": gla_b_gate,
            "gla_out_norm": gla_out_norm, "gla_w_out": gla_w_out,
            "gdn_w_in": gdn_w_in, "gdn_conv": gdn_conv, "gdn_a_log": gdn_a_log,
            "gdn_dt_bias": gdn_dt_bias, "gdn_out_norm": gdn_out_norm, "gdn_w_out": gdn_w_out,
            "ffn_norm": ffn_norm, "ffn_w_in": ffn_w_in, "ffn_w_out": ffn_w_out,
            "ple_norm": ple_norm, "ple_w_gate": ple_w_gate, "ple_w_proj": ple_w_proj,
            "final_norm": final_norm}

def first_block(x, p, mixer_norm, gla_w_in, gla_w_gate_up, gla_b_gate, gla_out_norm, gla_w_out,
              gdn_w_in, gdn_conv, gdn_a_log, gdn_dt_bias, gdn_out_norm, gdn_w_out,
              ffn_norm, ffn_w_in, ffn_w_out, ple_norm, ple_w_gate, ple_w_proj, final_norm):
    h = x
    for i in range(DEPTH):
        j = i // NUM_MIXERS
        hn = rmsnorm(h, mixer_norm[i])
        if i % NUM_MIXERS == 0:
            mix = gla_mixer(hn, gla_w_in[j], gla_w_gate_up[j], gla_b_gate[j],
                            gla_out_norm[j], gla_w_out[j])
        else:
            mix = gdn_mixer(hn, gdn_w_in[j], gdn_conv[j], gdn_a_log[j], gdn_dt_bias[j],
                            gdn_out_norm[j], gdn_w_out[j])
        h = h + mix
        h = h + swiglu(rmsnorm(h, ffn_norm[i]), ffn_w_in[i], ffn_w_out[i])
        gate = jax.nn.sigmoid(jnp.einsum('btd,de->bte', rmsnorm(h, ple_norm[i]), ple_w_gate[i]))
        h = h + gate * jnp.einsum('btk,kd->btd', p[i], ple_w_proj[i])
    return rmsnorm(h, final_norm)


MLSTM_HEADS = 8
MLSTM_WIDTH = D_MODEL
MLSTM_HEAD_DIM = MLSTM_WIDTH // MLSTM_HEADS
QK_CONV_WIDTH = 4
POOL_GROUPS = 4
POOL_WIDTH = D_MODEL // 2
POOL_GROUP_DIM = POOL_WIDTH // POOL_GROUPS
POOL_WINDOWS = (2, 4, 8, 16)
RMS_EPS = 1e-6
IN_SPLITS = (MLSTM_WIDTH, MLSTM_WIDTH, MLSTM_WIDTH, MLSTM_WIDTH, MLSTM_WIDTH,
             MLSTM_HEADS, MLSTM_HEADS, POOL_WIDTH, POOL_WIDTH, D_MODEL, D_MODEL)
IN_WIDTH = 5 * MLSTM_WIDTH + 2 * MLSTM_HEADS + 2 * POOL_WIDTH + 2 * D_MODEL


def _rmsnorm(x, w):
    xf = x.astype(jnp.float32)
    y = xf * lax.rsqrt(jnp.mean(xf * xf, axis=-1, keepdims=True) + RMS_EPS)
    return (y * w.astype(jnp.float32)).astype(x.dtype)

def _partition(t):
    parts, start = [], 0
    for width in IN_SPLITS:
        parts.append(t[..., start:start + width])
        start += width
    return parts

def _causal_depthwise_conv(x, w, b):
    c = x.shape[-1]
    y = lax.conv_general_dilated(
        x, w[:, None, :].astype(x.dtype), window_strides=(1,),
        padding=[(w.shape[0] - 1, 0)], dimension_numbers=('NWC', 'WIO', 'NWC'),
        feature_group_count=c)
    return y + b.astype(x.dtype)

def _to_chunks(t, nc):
    b = t.shape[0]
    t = t.reshape((b, nc, CHUNK) + t.shape[2:])
    t = jnp.moveaxis(t, 1, 0)
    return jnp.swapaxes(t, 2, 3)

def _mlstm_chunkwise(q, k, v, ig, lf):
    bsz, s, nh, d = q.shape
    nc = s // CHUNK
    causal = jnp.tril(jnp.ones((CHUNK, CHUNK), dtype=bool))
    xs = (_to_chunks(q, nc), _to_chunks(k, nc), _to_chunks(v, nc),
          _to_chunks(ig, nc), _to_chunks(lf, nc))

    def step(carry, inp):
        c_st, n_st, m_st = carry
        qc, kc, vc, ic, fc = inp
        b = jnp.cumsum(fc, axis=-1)
        log_d = b[..., :, None] - b[..., None, :] + ic[..., None, :]
        log_d = jnp.where(causal, log_d, -jnp.inf)
        log_inter = b + m_st[..., None]
        m_row = jnp.maximum(jnp.max(log_d, axis=-1), log_inter)
        p = jnp.exp(log_d - m_row[..., None]) * jnp.einsum('bhld,bhsd->bhls', qc, kc)
        w_inter = jnp.exp(log_inter - m_row)
        num = (jnp.einsum('bhls,bhsd->bhld', p, vc)
               + w_inter[..., None] * jnp.einsum('bhlk,bhkv->bhlv', qc, c_st))
        den = jnp.sum(p, axis=-1) + w_inter * jnp.einsum('bhlk,bhk->bhl', qc, n_st)
        h = num / jnp.maximum(jnp.abs(den), jnp.exp(-m_row))[..., None]
        g = b[..., -1]
        log_w = g[..., None] - b + ic
        m_new = jnp.maximum(g + m_st, jnp.max(log_w, axis=-1))
        decay = jnp.exp(g + m_st - m_new)
        w = jnp.exp(log_w - m_new[..., None])
        c_new = decay[..., None, None] * c_st + jnp.einsum('bhs,bhsk,bhsv->bhkv', w, kc, vc)
        n_new = decay[..., None] * n_st + jnp.einsum('bhs,bhsk->bhk', w, kc)
        return (c_new, n_new, m_new), h

    init = (jnp.zeros((bsz, nh, d, d), jnp.float32),
            jnp.zeros((bsz, nh, d), jnp.float32),
            jnp.zeros((bsz, nh), jnp.float32))
    _, hs = lax.scan(step, init, xs)
    hs = jnp.moveaxis(jnp.swapaxes(hs, 2, 3), 0, 1)
    return hs.reshape(bsz, s, nh, d)

def _multiscale_pool(u):
    bsz, s, _ = u.shape
    uf = u.astype(jnp.float32).reshape(bsz, s, POOL_GROUPS, POOL_GROUP_DIM)
    cs = jnp.concatenate(
        [jnp.zeros((bsz, 1, POOL_GROUPS, POOL_GROUP_DIM), jnp.float32),
         jnp.cumsum(uf, axis=1)], axis=1)
    t = jnp.arange(1, s + 1)[:, None]
    win = jnp.array(POOL_WINDOWS, dtype=jnp.int32)[None, :]
    lo = jnp.maximum(t - win, 0)
    grp = jnp.arange(POOL_GROUPS)[None, :]
    window_sum = cs[:, 1:] - cs[:, lo, grp]
    count = (t - lo).astype(jnp.float32)
    return window_sum / count[..., None] - uf

def second_inputs(seed: int = 0) -> dict:
    key = jax.random.key(seed)
    ks = jax.random.split(key, 16)
    f32 = jnp.float32
    nrm = lambda k, shape, scale: (jax.random.normal(k, shape, f32) * scale)
    x = jax.random.normal(ks[0], (BATCH, SEQ, D_MODEL), f32)
    norm_pre_w = 1.0 + nrm(ks[1], (DEPTH, D_MODEL), 0.05)
    w_in = nrm(ks[2], (DEPTH, D_MODEL, IN_WIDTH), D_MODEL ** -0.5)
    mlstm_i_bias = nrm(ks[3], (DEPTH, MLSTM_HEADS), 0.1)
    mlstm_f_bias = (jnp.linspace(3.0, 6.0, MLSTM_HEADS, dtype=f32)[None, :]
                    + nrm(ks[4], (DEPTH, MLSTM_HEADS), 0.1))
    qk_conv_w = nrm(ks[5], (DEPTH, QK_CONV_WIDTH, 2 * MLSTM_WIDTH), QK_CONV_WIDTH ** -0.5)
    qk_conv_b = nrm(ks[6], (DEPTH, 2 * MLSTM_WIDTH), 0.01)
    mlstm_norm_w = 1.0 + nrm(ks[7], (DEPTH, MLSTM_WIDTH), 0.05)
    pool_w = nrm(ks[8], (DEPTH, POOL_GROUPS, POOL_GROUP_DIM, POOL_GROUP_DIM), POOL_GROUP_DIM ** -0.5)
    pool_scale = 1.0 + nrm(ks[9], (DEPTH, POOL_WIDTH), 0.1)
    w_proj_mlstm = nrm(ks[10], (DEPTH, MLSTM_WIDTH, D_MODEL), MLSTM_WIDTH ** -0.5)
    w_proj_pool = nrm(ks[11], (DEPTH, POOL_WIDTH, D_MODEL), POOL_WIDTH ** -0.5)
    w_out = nrm(ks[12], (DEPTH, D_MODEL, D_MODEL), D_MODEL ** -0.5)
    norm_post_w = 1.0 + nrm(ks[13], (DEPTH, D_MODEL), 0.05)
    return {'x': x, 'norm_pre_w': norm_pre_w, 'w_in': w_in,
            'mlstm_i_bias': mlstm_i_bias, 'mlstm_f_bias': mlstm_f_bias,
            'qk_conv_w': qk_conv_w, 'qk_conv_b': qk_conv_b,
            'mlstm_norm_w': mlstm_norm_w, 'pool_w': pool_w, 'pool_scale': pool_scale,
            'w_proj_mlstm': w_proj_mlstm, 'w_proj_pool': w_proj_pool,
            'w_out': w_out, 'norm_post_w': norm_post_w}

def second_block(x, norm_pre_w, w_in, mlstm_i_bias, mlstm_f_bias, qk_conv_w, qk_conv_b,
              mlstm_norm_w, pool_w, pool_scale, w_proj_mlstm, w_proj_pool, w_out,
              norm_post_w):
    bsz, s, _ = x.shape
    f32 = jnp.float32
    for l in range(DEPTH):
        h = _rmsnorm(x, norm_pre_w[l])
        proj = jnp.einsum('bsd,de->bse', h, w_in[l])
        (q, k, v, o_g, z_a, i_pre, f_pre, u_b, z_b, g_a, g_b) = _partition(proj)

        qk = jax.nn.silu(_causal_depthwise_conv(jnp.concatenate([q, k], axis=-1),
                                                qk_conv_w[l], qk_conv_b[l]))
        q = qk[..., :MLSTM_WIDTH].astype(f32).reshape(bsz, s, MLSTM_HEADS, MLSTM_HEAD_DIM)
        k = qk[..., MLSTM_WIDTH:].astype(f32).reshape(bsz, s, MLSTM_HEADS, MLSTM_HEAD_DIM)
        v = v.astype(f32).reshape(bsz, s, MLSTM_HEADS, MLSTM_HEAD_DIM)
        q = q * (MLSTM_HEAD_DIM ** -0.5)
        log_i = i_pre.astype(f32) + mlstm_i_bias[l].astype(f32)
        log_f = jax.nn.log_sigmoid(f_pre.astype(f32) + mlstm_f_bias[l].astype(f32))
        h_t = _mlstm_chunkwise(q, k, v, log_i, log_f)
        h_t = h_t * lax.rsqrt(jnp.mean(h_t * h_t, axis=-1, keepdims=True) + RMS_EPS)
        h_t = h_t * mlstm_norm_w[l].astype(f32).reshape(MLSTM_HEADS, MLSTM_HEAD_DIM)
        h_a = jax.nn.sigmoid(o_g.astype(f32)) * h_t.reshape(bsz, s, MLSTM_WIDTH)
        y_a = (h_a * jax.nn.silu(z_a.astype(f32))).astype(x.dtype)

        pooled = _multiscale_pool(u_b)
        mixed = jnp.einsum('bsgc,gcd->bsgd', pooled, pool_w[l].astype(f32))
        mixed = mixed.reshape(bsz, s, POOL_WIDTH) * pool_scale[l].astype(f32)
        y_b = (mixed * jax.nn.silu(z_b.astype(f32))).astype(x.dtype)

        br_a = jnp.einsum('bsc,cd->bsd', y_a, w_proj_mlstm[l])
        br_b = jnp.einsum('bsc,cd->bsd', y_b, w_proj_pool[l])
        merged = jax.nn.sigmoid(g_a) * br_a + jax.nn.sigmoid(g_b) * br_b
        out = jnp.einsum('bsd,de->bse', merged, w_out[l])
        x = x + _rmsnorm(out, norm_post_w[l])
    return x


def setup_inputs(seed=0):
    out = dict(first_inputs(seed))
    for name, value in second_inputs(seed + 1).items():
        if name != "x":
            out[name + "_2"] = value
    return out


def reference(
    x, p, mixer_norm, gla_w_in, gla_w_gate_up, gla_b_gate, gla_out_norm, gla_w_out, gdn_w_in,
    gdn_conv, gdn_a_log, gdn_dt_bias, gdn_out_norm, gdn_w_out, ffn_norm, ffn_w_in, ffn_w_out,
    ple_norm, ple_w_gate, ple_w_proj, final_norm, norm_pre_w_2, w_in_2, mlstm_i_bias_2,
    mlstm_f_bias_2, qk_conv_w_2, qk_conv_b_2, mlstm_norm_w_2, pool_w_2, pool_scale_2,
    w_proj_mlstm_2, w_proj_pool_2, w_out_2, norm_post_w_2,
):
    x = first_block(
        x, p, mixer_norm, gla_w_in, gla_w_gate_up, gla_b_gate, gla_out_norm, gla_w_out,
        gdn_w_in, gdn_conv, gdn_a_log, gdn_dt_bias, gdn_out_norm, gdn_w_out, ffn_norm, ffn_w_in,
        ffn_w_out, ple_norm, ple_w_gate, ple_w_proj, final_norm,
    )
    return second_block(
        x, norm_pre_w_2, w_in_2, mlstm_i_bias_2, mlstm_f_bias_2, qk_conv_w_2, qk_conv_b_2,
        mlstm_norm_w_2, pool_w_2, pool_scale_2, w_proj_mlstm_2, w_proj_pool_2, w_out_2,
        norm_post_w_2,
    )


_drawn_inputs = setup_inputs


def setup_inputs(seed=0):
    import zlib

    import numpy as np

    out = dict(_drawn_inputs(seed))
    spreads = {}
    factors = {'ple_norm': 5.636, 'mlstm_i_bias_2': 64.0, 'qk_conv_b_2': 8.0, 'mlstm_norm_w_2': 3.043}
    for name, (base, spread) in spreads.items():
        noise = np.random.default_rng([zlib.crc32(name.encode()), seed]).standard_normal(out[name].shape)
        drawn = base * np.exp(spread * noise) if base else spread * noise
        out[name] = jnp.asarray(drawn.astype(out[name].dtype))
    for name, factor in factors.items():
        out[name] = (out[name] * factor).astype(out[name].dtype)
    return out
```

```python
from contextlib import ExitStack

import concourse.bass as bass
from concourse import mybir

F32 = mybir.dt.float32
F32R = mybir.dt.float32r
BF16 = mybir.dt.bfloat16
I8 = mybir.dt.int8
ACT = mybir.ActivationFunctionType
ALU = mybir.AluOpType
AX = mybir.AxisListType

P = 128
T = 256
D = 2048
EPS = 1e-6
DFF = 5632
HF = 256
NC = 512
RAW_SLOTS = 8
HL_SLOTS = 4
LAG = 3

GH, GDK, GDV = 4, 256, 512
GK = GH * GDK
RANK = 16
GATE_NORM = 16.0
LEVELS = [64, 32, 16, 8, 4, 2, 1]
UNITS = 2 * (1 + len(LEVELS))

MH, MD = 8, 256
VW = 258
POOL_WINDOWS = (2, 4, 8, 16)

VEC = {}
_at = 0
for _name, _rows in (("mixer_norm", 16), ("gla_out_norm", 4), ("ffn_norm", 16), ("ple_norm", 16),
                     ("final_norm", 16), ("norm_pre", 16), ("pool_scale", 8), ("mlstm_norm", 16)):
    VEC[_name] = (_at, _rows)
    _at += _rows
VEC_ROWS = _at


class Job:

    def __init__(self, name, n, granules, width=NC, per_granule=1):
        self.name, self.n, self.gr, self.w, self.dmas = name, n, granules, width, per_granule
        self.G = len(granules)


def granules(k_tiles, size=2):
    return [(k, min(size, k_tiles - k)) for k in range(0, k_tiles, size)]


def plan():
    full = granules(16)
    jobs = [
        Job("lr", 1, full, 2 * RANK), Job("qk", 4, full), Job("v", 4, full), Job("og", 4, full),
        Job("wo", 4, full),
        Job("f1", 12, full, NC, 2), Job("f1o", 4, granules(24)),
        Job("f2", 10, full, NC, 2), Job("f2o", 4, granules(20)),
        Job("pp", 4, granules(2)), Job("pg", 4, full),
        Job("ub", 2, full), Job("zb", 2, full), Job("pool", 4, granules(2, 1), 256),
        Job("if", 1, full, 2 * MH), Job("qk2", 8, full), Job("v2", 4, full),
        Job("oz", 8, full, NC, 2), Job("gb", 4, full), Job("ga", 4, full),
        Job("pb", 4, granules(8)), Job("pm", 4, full), Job("out", 4, full),
    ]
    tile = gran = 0
    landed = [0] * RAW_SLOTS
    for prev, job in zip([None] + jobs[:-1], jobs):
        job.prev, job.t0, job.g0, job.landed0 = prev, tile, gran, list(landed)
        tile += job.n
        for q in range(job.n * job.G):
            landed[(gran + q) % RAW_SLOTS] += 16 * job.dmas
        gran += job.n * job.G
    byname = {j.name: j for j in jobs}
    r = x = 0
    for name, n, split in (
            ("vec", 1, 0), ("x", 4, 1), ("lr", 1, 0), ("qk", 4, 0), ("o", 4, 0), ("y", 4, 1),
            ("wo", 4, 1), ("f1", 12, 1), ("f2", 10, 1), ("pt", 1, 1), ("f2o", 4, 1), ("pg", 4, 1),
            ("ub", 2, 1), ("pool", 4, 1), ("if", 2, 0), ("qk2", 8, 0), ("num", 8, 0), ("ya", 4, 1),
            ("pm", 4, 1)):
        if name not in byname:
            byname[name] = Job(name, n, [])
        byname[name].r0, byname[name].x0 = r, x
        r, x = r + n, x + 2 * n * split
    return jobs, byname


def build(nc, x, p, mixer_norm, gla_w_in, gla_w_gate_up, gla_b_gate, gla_out_norm, gla_w_out,
          ffn_norm, ffn_w_in, ffn_w_out, ple_norm, ple_w_gate, ple_w_proj, final_norm,
          norm_pre, w_in2, i_bias, f_bias, conv_w, conv_b, mlstm_norm, pool_w, pool_scale,
          w_mlstm, w_pool, w_out2, norm_post,
          c_ident, c_sums, c_masks, c_diag, c_windows, out):
    JOBS, J = plan()

    def rows(ap):
        return ap.rearrange("(k p) n -> p k n", p=P)

    gin, win = rows(gla_w_in), rows(w_in2)
    fin, fout = rows(ffn_w_in), rows(ffn_w_out)
    qkv_at = 5 * D + 2 * MH
    SRC = {
        "lr": (gin, lambda n: 2 * GK + 2 * D), "qk": (gin, lambda n: n * NC),
        "v": (gin, lambda n: 2 * GK + n * NC), "og": (gin, lambda n: 2 * GK + D + n * NC),
        "wo": (rows(gla_w_out), lambda n: n * NC),
        "f1": (fin, lambda n: n * HF), "f1o": (fout[:, 0:24, :], lambda n: n * NC),
        "f2": (fin, lambda n: (n + 12) * HF), "f2o": (fout[:, 24:44, :], lambda n: n * NC),
        "pp": (rows(ple_w_proj), lambda n: n * NC), "pg": (rows(ple_w_gate), lambda n: n * NC),
        "ub": (win, lambda n: qkv_at + n * NC), "zb": (win, lambda n: qkv_at + 1024 + n * NC),
        "pool": None,
        "if": (win, lambda n: 5 * D), "qk2": (win, lambda n: n * NC),
        "v2": (win, lambda n: 2 * D + n * NC), "oz": (win, lambda n: 3 * D + n * MD),
        "gb": (win, lambda n: qkv_at + 2048 + D + n * NC), "ga": (win, lambda n: qkv_at + 2048 + n * NC),
        "pb": (rows(w_pool), lambda n: n * NC), "pm": (rows(w_mlstm), lambda n: n * NC),
        "out": (rows(w_out2), lambda n: n * NC),
    }
    SECOND_HALF = {"f1": DFF, "f2": DFF, "oz": D}

    ctx = ExitStack()
    with ctx:
        base = (nc.sbuf_base + 63) // 64 * 64
        used_to = [base]

        def at(name, shape, dt, offset):
            return nc.alloc_sbuf_tensor_at(name, shape, dt, offset=offset)

        def own(name, shape, dt, size):
            offset = used_to[0]
            used_to[0] += (size + 31) // 32 * 32
            return at(name, shape, dt, offset), offset

        raw, _ = own("raw", [P, RAW_SLOTS, 2 * NC], F32, RAW_SLOTS * 4096)
        w_hi, _ = own("w_hi", [P, HL_SLOTS, 2 * NC], F32R, HL_SLOTS * 4096)
        w_lo, _ = own("w_lo", [P, HL_SLOTS, 2 * NC], F32R, HL_SLOTS * 4096)
        xa_hi, xa_at = own("xa_hi", [P, 16, T], F32R, 16384)
        xa_lo, _ = own("xa_lo", [P, 16, T], F32R, 16384)
        xb_hi, xb_at = own("xb_hi", [P, 16, T], F32R, 16384)
        xb_lo, _ = own("xb_lo", [P, 16, T], F32R, 16384)
        H, h_at = own("H", [P, 2, D], F32, 16384)
        ident, _ = own("ident", [P, P], F32, 512)
        vec, _ = own("vec", [P, VEC_ROWS], F32, 4 * VEC_ROWS)
        cbias, _ = own("cbias", [P, 32], F32, 128)
        cw, _ = own("cw", [P, P], F32, 512)
        ssq, _ = own("ssq", [P, 6, 2, 4], F32, 192)
        msq, _ = own("msq", [P, 8, 2], F32, 64)
        rstd, _ = own("rstd", [P, 8, 2], F32, 64)
        S2 = 6
        half, _ = own("half", [P, 16], F32, 64)
        hss, _ = own("hss", [P, 16], F32, 64)
        hms, _ = own("hms", [P, 16], F32, 64)
        hrs, _ = own("hrs", [P, 16], F32, 64)
        junk, _ = own("junk", [P, NC], BF16, 1024)
        ov = used_to[0]
        room = nc.sbuf_usable_end - ov

        V = at("V", [P, 2, D], F32, xb_at)
        G = at("G", [P, 2, 2, GK], F32, xb_at + 16384)
        sums_raw = at("sums_raw", [P, 18 * P], F32, xb_at)
        masks_raw = at("masks_raw", [P, 14, P], F32, xb_at + 16384)
        vec_raw = at("vec_raw", [P, 3, P], F32, xb_at + 12288)
        o = ov
        stage = at("stage", [P, 2, NC], F32, o); o += 4096
        gates_at = o
        gates = at("gates", [P, 2, NC], F32, o); o += 4096
        phase = o
        qkT = at("qkT", [P, 16, T], F32, o); o += 16384
        A_T = at("A_T", [P, 4, P], F32, o); o += 2048
        Ex = at("Ex", [P, 2, T], F32, o); o += 2048
        X = at("X", [P, 2, T], F32, o); o += 2048
        g_hi = at("g_hi", [P, 2, 2, GDK], F32R, gates_at)
        g_lo = at("g_lo", [P, 2, 2, GDK], F32R, o); o += 4096
        sums = at("sums", [P, 18, P], F32R, o); o += 18 * 512
        masks = at("masks", [P, 14, 2 * P], I8, o); o += 14 * 256
        wgu = at("wgu", [RANK + 1, 2, GK], F32, o); o += 8192
        lrT = at("lrT", [RANK + 1, 2, T], F32, o); o += 2048
        diag2 = at("diag2", [P, 2 * P], F32, o); o += 1024
        assert o - ov <= room, (o - ov, room)
        xagain = at("xagain", [P, 2, D], F32, phase)
        o = phase
        hid_hi = at("hid_hi", [P, 24, T], F32R, o); o += 24576
        hid_lo = at("hid_lo", [P, 24, T], F32R, o); o += 24576
        assert o - ov <= room, (o - ov, room)
        pT_hi = at("pT_hi", [P, 2, T], F32R, phase + 20 * 1024)
        pT_lo = at("pT_lo", [P, 2, T], F32R, phase + 24576 + 20 * 1024)
        p_tok = at("p_tok", [P, 2, T], F32, gates_at)
        PPJ = at("PPJ", [P, 2, D], F32, phase)
        fn_bc = at("fn_bc", [P, D], F32, phase + 24576)
        o = phase
        GB = at("GB", [P, 2, D], F32, o)
        windows = at("windows", [P, 4, 384], F32, o)
        small = o + 8192
        o += 16384
        U = at("U", [P, 2, 1024], F32, o)
        ZB = at("ZB", [P, 2, 1024], F32, o + 8192)
        VA = at("VA", [P, 2, MH, VW], F32, o)
        GA = at("GA", [P, 2, D], F32, o); o += 2 * MH * VW * 4
        yb_hi = at("yb_hi", [P, 8, T], F32R, o)
        npw_bc = at("npw_bc", [P, D], F32, o); o += 8192
        yb_lo = at("yb_lo", [P, 8, T], F32R, o); o += 8192
        W = at("W", [P, 384], F32, o); o += 1536
        PT = at("PT", [P, 384], F32, o); o += 1536
        aR = at("aR", [MH, T], F32, o); o += 1024
        bT = at("bT", [P, 2, MH], F32, o); o += 64
        emT = at("emT", [P, 2, MH], F32, o); o += 64
        den = at("den", [P, 2], F32, o); o += 32
        rden = at("rden", [P, 2], F32, o); o += 32
        assert o - ov <= room, (o - ov, room)
        qk2T = at("qk2T", [P, 32, T], F32, xa_at)
        conv = at("conv", [P, 4, T], F32, gates_at)
        gate_bias = at("gate_bias", [P, 2 * MH], F32, small)
        gi = at("gi", [P, 2, 2 * MH], F32, small + 64)
        minus_abs_f = at("minus_abs_f", [P, 2, MH], F32, small + 192)
        lnf = at("lnf", [P, 2, MH], F32, small + 256)
        logf = at("logf", [P, 2, MH], F32, small + 320)
        iR = at("iR", [MH, T], F32, small + 1024)
        fR = at("fR", [MH, T], F32, small + 2048)
        ones8 = at("ones8", [MH, T], F32, small + 3072)
        Fc = at("Fc", [MH, T], F32, small + 4096)
        mR = at("mR", [MH, T], F32, small + 5120)
        bR = at("bR", [MH, T], F32, small + 6144)
        emR = at("emR", [MH, T], F32, small + 7168)
        OUT = at("OUT", [P, 2, D], F32, xa_at)

        acc = [[ctx.enter_context(nc.psum_tensor(f"acc{a}{b}", [P, NC], F32)) for b in range(2)]
               for a in range(2)]
        tp = [ctx.enter_context(nc.psum_tensor(f"tp{b}", [P, NC], F32)) for b in range(2)]
        mx = [ctx.enter_context(nc.psum_tensor(f"mx{b}", [P, NC], F32)) for b in range(2)]

        def sem(name):
            return ctx.enter_context(nc.semaphore(name))

        landed = [sem(f"landed{i}") for i in range(RAW_SLOTS)]
        hi_ready, lo_ready, consumed = sem("hi_ready"), sem("lo_ready"), sem("consumed")
        evac = [sem("evac0"), sem("evac1")]
        tp_ready = sem("tp_ready")
        tp_read = [sem("tp_read0"), sem("tp_read1")]
        xt_hi = sem("xt_hi")
        ms_ready, rstd_ready, squared = sem("ms_ready"), sem("rstd_ready"), sem("squared")
        loads = {k: sem(f"load_{k}") for k in (
            "x", "ident", "vec", "sums", "masks", "diag", "wgu", "xagain", "p", "fn", "windows", "gbias",
            "npw", "out")}
        act_self, dve_self = sem("act_self"), sem("dve_self")
        half_set, ones_row_set, ones_set = sem("half_set"), sem("ones_row_set"), sem("ones_set")
        sums_ready, masks_ready = sem("sums_ready"), sem("masks_ready")
        gk_ready, gk_read, gk_min, gk_exp, gk_ln, g_ready = (
            sem("gk_ready"), sem("gk_read"), sem("gk_min"), sem("gk_exp"), sem("gk_ln"), sem("g_ready"))
        gsplit_hi, gsplit_lo = sem("gsplit_hi"), sem("gsplit_lo")
        e_ready, ex_ready, xq_ready, xk_ready = sem("e_ready"), sem("ex_ready"), sem("xq_ready"), sem("xk_ready")
        p_ready, a_ready = sem("p_ready"), sem("a_ready")
        ho_ms, ho_rstd = sem("ho_ms"), sem("ho_rstd")
        f_gate = sem("f_gate")
        sgp_ready, h_ready = sem("sgp_ready"), sem("h_ready")
        hf_ready = [sem("hf_ready0"), sem("hf_ready1")]
        s2_ready = sem("s2_ready")
        abs_ready, ln_ready, logf_ready, scan_ready, em_ready = (
            sem("abs_ready"), sem("ln_ready"), sem("logf_ready"), sem("scan_ready"), sem("em_ready"))
        qk2_ready = sem("qk2_ready")
        oz_sg, oz_prod = sem("oz_sg"), sem("oz_prod")
        s_ready, w_ready, wexp_ready, wmask_ready, pt_ready = (
            sem("s_ready"), sem("w_ready"), sem("wexp_ready"), sem("wmask_ready"), sem("pt_ready"))
        ya_ready = [sem("ya_ready0"), sem("ya_ready1")]
        merged_ready = [sem("merged_ready0"), sem("merged_ready1")]
        x2_ready, y_ready = sem("x2_ready"), sem("y_ready")

        block = ctx.enter_context(nc.Block())

        def gran(job, n, j):
            return job.g0 + n * job.G + j

        def width(job, kc):
            return kc * job.w

        def cols(n, size=NC):
            return slice(n * size, (n + 1) * size) if isinstance(n, int) else bass.ds(n * size, size)

        def acc_of(job, ns):
            return acc[(job.t0 + ns) % 2]

        def done(job, n):
            return gran(job, n + 1, 0)

        def E(job, n):
            return job.t0 + n + 1

        def JE(job):
            return min(3, job.G - 1)

        def JT(job, prev_name):
            return min(5 if prev_name == "pg" else 3, job.G - 1)

        def JV(job, prev_name):
            return min(7 if prev_name == "pg" else 6, job.G - 1)

        def vcol(name, k):
            a = VEC[name][0] + k
            return vec[:, a:a + 1]

        NORM_OF = {"x": "mixer_norm", "wo": "ffn_norm", "f2o": "ple_norm",
                   "pg": "norm_pre", "ya": "mlstm_norm", "pool": "pool_scale", "y": "gla_out_norm"}
        DEST = {"x": (xa_hi, xa_lo), "y": (xa_hi, xa_lo), "wo": (xb_hi, xb_lo), "f2o": (xa_hi, xa_lo),
                "pg": (xb_hi, xb_lo), "ub": (xa_hi, xa_lo), "ya": (xa_hi, xa_lo), "pm": (xb_hi, xb_lo),
                "pool": (yb_hi, yb_lo), "pt": (pT_hi, pT_lo), "f1": (hid_hi, hid_lo), "f2": (hid_hi, hid_lo)}

        def xt_part(job, part, k):
            src = {"f1o": "f1", "f2o": "f2", "lr": "x", "qk": "x", "v": "x", "og": "x", "wo": "y", "f1": "wo", "f2": "wo",
                   "pp": "pt", "pg": "f2o", "ub": "pg", "zb": "pg", "pool": "ub", "if": "pg",
                   "qk2": "pg", "v2": "pg", "oz": "pg", "gb": "pg", "ga": "pg", "pb": "pool",
                   "pm": "ya", "out": "pm"}[job.name]
            return DEST[src][part][:, k, :]

        def needs(job, j):
            name = job.name
            by_bank = {"lr": "x", "wo": "y", "f1": "wo", "pg": "f2o", "ub": "pg", "out": "pm"}
            if name in by_bank:
                return [(J[by_bank[name]].r0 + j // 2, j % 2)]
            by_round = {"f1o": J["f1"].r0 + j, "f2o": J["f2"].r0 + j, "pp": J["pt"].r0,
                        "pool": J["ub"].r0 + 1, "pb": J["pool"].r0 + 3, "pm": J["ya"].r0 + 3}
            if name in by_round:
                return [(by_round[name], 0), (by_round[name], 1)]
            return []

        def unit(u):
            d, lv = divmod(u, 1 + len(LEVELS))
            return d, lv - 1

        def unit_rows(u):
            d, lv = unit(u)
            l = P if lv < 0 else LEVELS[lv]
            return (1, 0, l) if d == 0 else (0, 1, l)

        def halves(ap, which, l):
            if l == P:
                return ap[:, :, which * P:(which + 1) * P]
            return ap.rearrange("p c (b two l) -> p c b two l", two=2, l=l)[:, :, :, which, :]

        def a_block(jt, it):
            return jt if jt == it else 2 + jt

        def loop_passes(job):
            return (job.n - 2) // 2

        LOOPED = ("f1", "f2")

        SQ = {"x": 0, "gla": 8, "wo": 8 + 2 * GH, "f2o": 16 + 2 * GH, "pg": 24 + 2 * GH,
              "mlstm": 40 + 2 * GH, "out": 40 + 2 * GH + 2 * MH}

        @block.sync
        def _(sp):
            sp.dma_start(ident[:, :], c_ident).then_inc(loads["ident"], 16)
            sp.dma_start(H[:, :, :], x[0].rearrange("(t p) d -> p t d", p=P)).then_inc(loads["x"], 16)

            def load(job, n, j, ns):
                g = gran(job, n, j)
                k0, kc = job.gr[j]
                slot = (job.g0 + ns * job.G + j) % RAW_SLOTS
                if not (isinstance(g, int) and g < RAW_SLOTS):
                    sp.wait_ge(lo_ready, g - RAW_SLOTS + 1)
                dst = raw[:, slot, 0:kc * job.w].rearrange("p (k n) -> p k n", k=kc)
                if job.name == "pool":
                    sp.dma_start(dst, pool_w[0, n, k0 * P:(k0 + 1) * P, :].rearrange("(k p) c -> p k c", p=P)) \
                        .then_inc(landed[slot], 16)
                    return
                src, first = SRC[job.name]
                if job.dmas == 2:
                    for a in range(2):
                        c = first(n) + a * SECOND_HALF[job.name]
                        sp.dma_start(dst[:, :, a * HF:(a + 1) * HF],
                                     src[:, k0:k0 + kc, bass.ds(c, HF)]).then_inc(landed[slot], 16)
                else:
                    sp.dma_start(dst, src[:, k0:k0 + kc, bass.ds(first(n), job.w)]) \
                        .then_inc(landed[slot], 16)

            for job in JOBS:
                if job.name in LOOPED:
                    for j in range(job.G):
                        load(job, 0, j, 0)
                    with sp.Fori(0, loop_passes(job)) as i:
                        for b in (1, 2):
                            for j in range(job.G):
                                load(job, 2 * i + b, j, b)
                    for j in range(job.G):
                        load(job, job.n - 1, j, job.n - 1)
                else:
                    for n in range(job.n):
                        for j in range(job.G):
                            load(job, n, j, n)
            for n in range(4):
                for t in range(2):
                    sp.wait_ge(y_ready, 2 * n + t + 1)
                    sp.dma_start(out[0, t * P:(t + 1) * P, cols(n)], OUT[:, t, cols(n)]) \
                        .then_inc(loads["out"], 16)
            sp.wait_ge(loads["out"], 16 * 8)

        @block.gpsimd
        def _(pool):
            nc.gpsimd.memset(half[:, :], -0.5).then_inc(half_set, 1)
            nc.gpsimd.memset(lrT[:, :, :], 1.0).then_inc(ones_row_set, 1)
            pool.wait_ge(half_set, 1)

            def inverse_root(i):
                pool.wait_ge(ms_ready, i + 1)
                nc.gpsimd.tensor_tensor(rstd[:, i, :], msq[:, i, :], half[:, 0:2], ALU.pow) \
                    .then_inc(rstd_ready, 1)

            pool.wait_ge(loads["masks"], 16)
            for t in range(2):
                nc.gpsimd.tensor_copy(masks[:, :, t * P:(t + 1) * P], masks_raw[:, :, :]) \
                    .then_inc(masks_ready, 1)

            inverse_root(0)
            for h in range(GH):
                for u in range(UNITS):
                    _, k_half, l = unit_rows(u)
                    n = h * UNITS + u
                    pool.wait_ge(ex_ready, n + 1)
                    if n == 0:
                        for b in range(2):
                            pool.wait_ge(tp_read[b], J["qk"].r0 + 4)
                    if u:
                        pool.wait_ge(p_ready, h * (UNITS + 1) + u + 1)
                    elif h:
                        pool.wait_ge(p_ready, h * (UNITS + 1))
                    nc.gpsimd.tensor_tensor(
                        halves(X[:, :, :], k_half, l), halves(qkT[:, 8 + 2 * h:10 + 2 * h, :], k_half, l),
                        halves(Ex[:, :, :], k_half, l), ALU.mult).then_inc(xk_ready, 1)
                pool.wait_ge(ho_ms, h + 1)
                nc.gpsimd.tensor_tensor(hrs[:, 2 * h:2 * h + 2], hms[:, 2 * h:2 * h + 2], half[:, 0:2],
                                        ALU.pow).then_inc(ho_rstd, 1)
            inverse_root(1)
            inverse_root(2)
            for n in range(4):
                for t in range(2):
                    pool.wait_ge(evac[t], E(J["pg"], n))
                nc.gpsimd.tensor_tensor(gates[:, :, :], gates[:, :, :], PPJ[:, :, cols(n)], ALU.mult) \
                    .then_inc(sgp_ready, 1)
            inverse_root(3)
            inverse_root(4)
            pool.wait_ge(rstd_ready, 4)
            pool.wait_ge(tp_ready, 2 * (J["pg"].r0 + 4))
            pool.wait_ge(squared, SQ["pg"] + 16)
            for t in range(2):
                nc.gpsimd.tensor_scalar(H[:, t, :], H[:, t, :], rstd[:, 3, t:t + 1], None, ALU.mult) \
                    .then_inc(x2_ready, 1)
            for t in range(2):
                pool.wait_ge(evac[t], E(J["pool"], 3))
            nc.gpsimd.memset(VA[:, :, :, MD:VW], 1.0).then_inc(ones_set, 1)
            nc.gpsimd.memset(ones8[:, :], 1.0).then_inc(ones_set, 1)
            for h in range(MH):
                pool.wait_ge(wexp_ready, h + 1)
                for c in (0, T):
                    nc.gpsimd.affine_select(out=W[:, c:c + P], in_=W[:, c:c + P], compare_op=ALU.is_ge,
                                            fill=0.0, base=0, pattern=[[1, P]], channel_multiplier=-1) \
                        .then_inc(wmask_ready, 1)
            pool.wait_ge(ho_ms, GH + 1)
            nc.gpsimd.tensor_tensor(hrs[:, :], hms[:, :], half[:, :], ALU.pow).then_inc(ho_rstd, 1)
            inverse_root(5)

        @block.scalar
        def _(act):
            def split_hi(job, n, j, ns):
                g = gran(job, n, j)
                kc = job.gr[j][1]
                sg = job.g0 + ns * job.G + j
                slot, hl = sg % RAW_SLOTS, sg % HL_SLOTS
                visit = n if job.name in LOOPED else (n * job.G + j) // RAW_SLOTS
                act.wait_ge(landed[slot], visit * (16 * job.dmas) + job.landed0[slot] + 16 * job.dmas)
                if not (isinstance(g, int) and g < HL_SLOTS):
                    act.wait_ge(consumed, g - HL_SLOTS + 1)
                nc.scalar.copy(w_hi[:, hl, 0:kc * job.w], raw[:, slot, 0:kc * job.w]).then_inc(hi_ready, 1)

            def xt_high(name, n, k_of, scale, full):
                r = J[name].r0 + n
                hi = DEST[name][0]
                for b in range(2):
                    act.wait_ge(tp_ready, 2 * r + b + 1)
                    k = k_of(b)
                    if scale is None:
                        ins = nc.scalar.copy(hi[:, bass.ds(k, full), :],
                                             tp[b][:, 0:full * T].rearrange("p (k t) -> p k t", k=full))
                    else:
                        for f in range(full):
                            ins = nc.scalar.activation(hi[:, k + f, :], tp[b][:, f * T:(f + 1) * T],
                                                       ACT.Copy, scale=scale(k + f))
                    ins.then_inc(xt_hi, 1)

            def squares(i, dst, src):
                if i:
                    act.wait_ge(squared, i)
                nc.scalar.activation(junk[:, 0:src.shape[-1]], src, ACT.Square, accum_out=dst) \
                    .then_inc(squared, 1)

            def evacuate(job, n, ns):
                name = job.name
                a = acc_of(job, ns)
                if name in ("f1o", "pool", "if", "pb", "pm"):
                    return
                act.wait_ge(consumed, done(job, n))
                if name in ("lr", "qk", "v", "qk2", "v2", "ub", "pp"):
                    w = job.w
                    scale = None if name == "pp" else rstd[:, 0 if name in ("lr", "qk", "v") else S2, 0:1]
                    dst = {"lr": stage, "qk": stage, "qk2": stage, "v": V, "v2": VA, "ub": U, "pp": PPJ}[name]
                    src = a[0][:, 0:w]
                    if name == "lr":
                        act.wait_ge(rstd_ready, 1)
                    if name in ("qk", "qk2"):
                        act.wait_ge(tp_ready, 2 * (job.r0 + n))
                    if name == "v":
                        act.wait_ge(g_ready, 8)
                    if name == "ub":
                        act.wait_ge(s2_ready, 1)
                        act.wait_ge(hf_ready[1], 4)
                    if name == "v2":
                        dst, src = dst[:, 0, 2 * n:2 * n + 2, 0:MD], src.rearrange("p (h d) -> p h d", h=2)
                    elif dst is stage:
                        dst = dst[:, 0, 0:w]
                    else:
                        dst = dst[:, 0, cols(n)]
                    if scale is None:
                        nc.scalar.copy(dst, src).then_inc(evac[0], 1)
                    else:
                        nc.scalar.activation(dst, src, ACT.Copy, scale=scale).then_inc(evac[0], 1)
                elif name in ("og", "zb"):
                    dst, i = (H, 0) if name == "og" else (ZB, S2)
                    for t in range(2):
                        nc.scalar.activation(dst[:, t, cols(n)], a[t][:, :], ACT.Silu,
                                             scale=rstd[:, i, t:t + 1]).then_inc(evac[t], 1)
                elif name in ("f1", "f2"):
                    act.wait_ge(rstd_ready, 2)
                    for t in range(2):
                        act.wait_ge(evac[t], E(job, n) - 1)
                        nc.scalar.activation(gates[:, t, 0:HF], a[t][:, 0:HF], ACT.Silu,
                                             scale=rstd[:, 1, t:t + 1]).then_inc(f_gate, 1)
                elif name in ("wo", "f2o"):
                    for t in range(2):
                        act.wait_ge(evac[t], E(job, n))
                        squares(SQ[name] + 2 * n + t, ssq[:, 1 if name == "wo" else 2, t, n:n + 1],
                                H[:, t, cols(n)])
                elif name == "pg":
                    act.wait_ge(rstd_ready, 3)
                    for t in range(2):
                        if n:
                            act.wait_ge(h_ready, 2 * n)
                        nc.scalar.activation(gates[:, t, :], a[t][:, :], ACT.Sigmoid,
                                             scale=rstd[:, 2, t:t + 1]).then_inc(evac[t], 1)
                elif name == "oz":
                    if n == 0:
                        act.wait_ge(qk2_ready, 16)
                    for t in range(2):
                        act.wait_ge(evac[t], E(job, n) - 1)
                        nc.scalar.activation(gates[:, t, :], a[t][:, :], ACT.Sigmoid,
                                             scale=rstd[:, S2, t:t + 1]).then_inc(oz_sg, 1)
                elif name in ("gb", "ga"):
                    dst = GB if name == "gb" else GA
                    for t in range(2):
                        act.wait_ge(ya_ready[t], n + 1 if name == "gb" else 4)
                        nc.scalar.activation(dst[:, t, cols(n)], a[t][:, :], ACT.Sigmoid,
                                             scale=rstd[:, S2, t:t + 1]).then_inc(evac[t], 1)
                elif name == "out":
                    for t in range(2):
                        squares(SQ["out"] + 2 * n + t, ssq[:, 5, t, n:n + 1], a[t][:, :])

            def evacuate_transposed(job, n):
                name = job.name
                if name == "lr":
                    act.wait_ge(tp_ready, 2 * job.r0 + 1)
                    act.wait_ge(ones_row_set, 1)
                    nc.scalar.copy(lrT[0:RANK, 0, :], tp[0][0:RANK, 0:T]).then_inc(tp_read[0], 1)
                elif name == "qk":
                    act.wait_ge(tp_ready, 2 * (job.r0 + n) + 1)
                    nc.scalar.activation(qkT[:, 4 * n:4 * n + 2, :],
                                         tp[0][:, :].rearrange("p (k t) -> p k t", k=2), ACT.Copy,
                                         scale=GDK ** -0.5 if n < 2 else 1.0).then_inc(tp_read[0], 1)
                elif name in ("wo", "f2o", "pg"):
                    xt_high(name, n, lambda b: 4 * n + 2 * b, lambda k: vcol(NORM_OF[name], k), 2)
                elif name in ("ub", "pm"):
                    xt_high(name, n, lambda b: 4 * n + 2 * b, None, 2)
                elif name in ("f1", "f2"):
                    xt_high(name, n, lambda b: 2 * n + b, None, 1)
                elif name == "pool":
                    xt_high(name, n, lambda b: 2 * n + b, lambda k: vcol("pool_scale", k), 1)

            def qk2_silu(n):
                for b in range(2):
                    act.wait_ge(tp_read[b], J["qk2"].r0 + n + 1)
                    nc.scalar.activation(qk2T[:, 4 * n + 2 * b:4 * n + 2 * b + 2, :],
                                         conv[:, 2 * b:2 * b + 2, :], ACT.Silu).then_inc(qk2_ready, 1)

            def gk_exp_of(i):
                t, z, c = i // 4, (i // 2) % 2, i % 2
                act.wait_ge(gk_read, i + 1)
                nc.scalar.activation(G[:, t, z, cols(c)], G[:, t, z, cols(c)], ACT.Exp) \
                    .then_inc(gk_exp, 1)

            def gk_ln_of(i):
                t, z, c = i // 4, (i // 2) % 2, i % 2
                act.wait_ge(gk_exp, i + 1)
                nc.scalar.activation(G[:, t, z, cols(c)], G[:, t, z, cols(c)], ACT.Ln, bias=1.0) \
                    .then_inc(gk_ln, 1)

            def gla_split(h):
                act.wait_ge(g_ready, 8)
                if h:
                    act.wait_ge(e_ready, UNITS * h)
                for t in range(2):
                    nc.scalar.copy(g_hi[:, t, :, :], G[:, t, :, h * GDK:(h + 1) * GDK]).then_inc(gsplit_hi, 1)

            def gla_exp(h, u):
                n = h * UNITS + u
                act.wait_ge(e_ready, n + 1)
                if n:
                    act.wait_ge(xq_ready, n)
                    act.wait_ge(xk_ready, n)
                nc.scalar.activation(Ex[:, :, :], mx[0][:, :].rearrange("p (c t) -> p c t", c=2), ACT.Exp,
                                     scale=1.0 / GATE_NORM).then_inc(ex_ready, 1)

            def gla_squares(h):
                for t in range(2):
                    act.wait_ge(tp_ready, 2 * (J["o"].r0 + h) + t + 1)
                    squares(SQ["gla"] + 2 * h + t, hss[:, 2 * h + t:2 * h + t + 1], tp[t][:, :])

            def mlstm_squares(h):
                for t in range(2):
                    act.wait_ge(tp_read[t], J["num"].r0 + h + 1)
                    squares(SQ["mlstm"] + 2 * h + t, hss[:, 2 * h + t:2 * h + t + 1], VA[:, t, h, 0:MD])

            def after_split(job, n, j, ns):
                name = job.name
                pj, pn, pns = (job.prev, job.prev.n - 1 if job.prev else 0, job.prev.n - 1 if job.prev else 0) \
                    if ns == 0 else (job, n - 1, ns - 1)
                if name == "qk" and n == 2:
                    gk_exp_of(j)
                if name == "qk" and n == 3:
                    gk_ln_of(j)
                if name == "og" and j >= LAG:
                    if j == LAG:
                        gla_split(n)
                    gla_exp(n, 2 * (j - LAG))
                    gla_exp(n, 2 * (j - LAG) + 1)
                if (name == "og" and n >= 1 or name == "wo" and n == 0) and j < LAG:
                    h = n - 1 if name == "og" else GH - 1
                    gla_exp(h, 2 * (j - LAG + 8))
                    gla_exp(h, 2 * (j - LAG + 8) + 1)
                    if j == LAG - 1:
                        gla_squares(h)
                if name == "qk2" and n >= 2 and j == 0:
                    qk2_silu(n - 2)
                if name == "v2" and n < 2 and j == 0:
                    qk2_silu(6 + n)
                if name == "oz" and n >= 1 and j == 1:
                    mlstm_squares(n - 1)
                if name == "gb" and n == 0 and j == 1:
                    mlstm_squares(MH - 1)
                if name == "oz" and j == 4:
                    act.wait_ge(w_ready, n + 1)
                    nc.scalar.activation(W[:, :], W[:, :], ACT.Exp).then_inc(wexp_ready, 1)
                if pj is not None and j == JE(job):
                    evacuate(pj, pn, pns)
                if pj is not None and pj.name == "pg" and j == 5:
                    for t in range(2):
                        act.wait_ge(h_ready, 2 * pn + t + 1)
                        squares(SQ["pg"] + 4 * pn + t, ssq[:, 3, t, pn:pn + 1], H[:, t, cols(pn)])
                if pj is not None and pj.name == "pg" and j == 6:
                    for t in range(2):
                        act.wait_ge(hf_ready[t], pn + 1)
                        squares(SQ["pg"] + 4 * pn + 2 + t, ssq[:, 4, t, pn:pn + 1], H[:, t, cols(pn)])
                if name == "f2o" and n == 1 and j == JV(job, "") - 1:
                    xt_high("pt", 0, lambda b: b, None, 1)
                if pj is not None and j == JV(job, pj.name):
                    evacuate_transposed(pj, pn)
                if name == "wo" and n == 0 and j in (3, 4, 5):
                    for h in {3: (0, 1), 4: (2,), 5: (3,)}[j]:
                        xt_high("y", h, lambda b: 4 * h + 2 * b, lambda k: vcol("gla_out_norm", k % 4), 2)
                if name == "gb" and j == 7:
                    xt_high("ya", n, lambda b: 4 * n + 2 * b, lambda k: vcol("mlstm_norm", k), 2)
                if name == "qk2" and n == 0 and j == 4:
                    act.wait_ge(abs_ready, 1)
                    nc.scalar.activation(lnf[:, :, :], minus_abs_f[:, :, :], ACT.Exp).then_inc(act_self, 1)
                    act.wait_ge(act_self, 1)
                    nc.scalar.activation(lnf[:, :, :], lnf[:, :, :], ACT.Ln, bias=1.0).then_inc(ln_ready, 1)
                if name == "qk2" and n == 0 and j == 5:
                    act.wait_ge(scan_ready, 1)
                    nc.scalar.activation(emR[:, :], mR[:, :], ACT.Exp, scale=-1.0).then_inc(em_ready, 1)
                if name == "wo" and n == 0 and j == 7:
                    act.wait_ge(p_ready, GH * (UNITS + 1))
                    act.wait_ge(xq_ready, GH * UNITS)
                    act.wait_ge(xk_ready, GH * UNITS)
                    act.dma_start(xagain[:, :, :], x[0].rearrange("(t p) d -> p t d", p=P)) \
                        .then_inc(loads["xagain"], 16)
                if name == "f2o" and n == 0 and j == job.G - 1:
                    for t in range(2):
                        act.wait_ge(evac[t], E(J["f2"], 9))
                    act.dma_start(p_tok[:, :, :], p[0, 0].rearrange("(t p) d -> p t d", p=P)) \
                        .then_inc(loads["p"], 16)
                if name == "pp" and n == 1:
                    act.wait_ge(consumed, done(J["f2o"], 3))
                    act.dma_start(fn_bc[:, :], final_norm.rearrange("(a d) -> a d", a=1)
                                  .broadcast_to([P, D])).then_inc(loads["fn"], 16)
                if name == "ub" and n == 0 and j == 7:
                    act.wait_ge(sgp_ready, 4)
                    act.dma_start(windows[:, :, :], c_windows.rearrange("p (g t) -> p g t", g=4)) \
                        .then_inc(loads["windows"], 16)
                    act.dma_start(gate_bias[:, 0:MH], i_bias.broadcast_to([P, MH])) \
                        .then_inc(loads["gbias"], 16)
                    act.dma_start(gate_bias[:, MH:2 * MH], f_bias.broadcast_to([P, MH])) \
                        .then_inc(loads["gbias"], 16)
                if name == "pm" and n == 0 and j == 0:
                    act.wait_ge(consumed, done(J["pb"], 3))
                    act.dma_start(npw_bc[:, :], norm_post.broadcast_to([P, D])).then_inc(loads["npw"], 16)

            act.dma_start(vec_raw[:, 0, :], conv_w[0].rearrange("w (f p) -> (w f) p", p=P)) \
                .then_inc(loads["vec"], 16)
            at_row = 0
            for ap in (mixer_norm, gla_out_norm, ffn_norm, ple_norm, final_norm, norm_pre, pool_scale,
                       mlstm_norm):
                flat = ap if len(ap.shape) == 1 else ap[0]
                n = flat.shape[0] // P
                act.dma_start(vec_raw[at_row:at_row + n, 1, :], flat.rearrange("(f p) -> f p", p=P)) \
                    .then_inc(loads["vec"], 16)
                at_row += n
            act.dma_start(vec_raw[0:32, 2, :], conv_b[0].rearrange("(f p) -> f p", p=P)) \
                .then_inc(loads["vec"], 16)
            act.dma_start(wgu[0:RANK, :, :], gla_w_gate_up[0].rearrange("z r d -> r z d")) \
                .then_inc(loads["wgu"], 16)
            act.dma_start(wgu[RANK:RANK + 1, :, :], gla_b_gate).then_inc(loads["wgu"], 16)
            act.dma_start(sums_raw[:, :], c_sums).then_inc(loads["sums"], 16)
            act.dma_start(masks_raw[:, :, :], c_masks.rearrange("p (a i) -> p a i", a=14)) \
                .then_inc(loads["masks"], 16)
            act.dma_start(diag2[:, :], c_diag).then_inc(loads["diag"], 16)
            act.wait_ge(loads["x"], 16)
            for n in range(4):
                for t in range(2):
                    squares(SQ["x"] + 2 * n + t, ssq[:, 0, t, n:n + 1], H[:, t, cols(n)])
            act.wait_ge(tp_read[1], 1)
            for r in range(4):
                xt_high("x", r, lambda b: 4 * r + 2 * b, lambda k: vcol("mixer_norm", k), 2)
                if r == 1:
                    for j in range(HL_SLOTS):
                        split_hi(J["lr"], 0, j, 0)
            act.wait_ge(loads["sums"], 16)
            nc.scalar.copy(sums[:, :, :], sums_raw[:, :].rearrange("p (a b) -> p a b", b=P)) \
                .then_inc(sums_ready, 1)

            for job in JOBS:
                def column_tile(n, ns):
                    for j in range(job.G):
                        if not (job.name == "lr" and j < HL_SLOTS):
                            split_hi(job, n, j, ns)
                        after_split(job, n, j, ns)
                if job.name in LOOPED:
                    column_tile(0, 0)
                    with act.Fori(0, loop_passes(job)) as i:
                        for b in (1, 2):
                            column_tile(2 * i + b, b)
                    column_tile(job.n - 1, job.n - 1)
                else:
                    for n in range(job.n):
                        column_tile(n, n)
            evacuate(J["out"], 3, 3)

        @block.tensor
        def _(pe):
            def product(job, n, j, ns):
                g = gran(job, n, j)
                k0, kc = job.gr[j]
                hl = (job.g0 + ns * job.G + j) % HL_SLOTS
                w = job.w
                a = acc_of(job, ns)
                if j == 0 and not (isinstance(n, int) and job.t0 + n < 2):
                    for t in range(2):
                        pe.wait_ge(evac[t], E(job, n) - 2)
                if ns == 0:
                    for r, b in needs(job, j):
                        pe.wait_ge(tp_read[b], r + 1)
                pe.wait_ge(lo_ready, g + 1)
                for kk in range(kc):
                    k = k0 + kk
                    kx = 2 * n + k if job.name == "pool" else k
                    hi = w_hi[:, hl, kk * w:(kk + 1) * w]
                    lo = w_lo[:, hl, kk * w:(kk + 1) * w]
                    first = j == 0 and kk == 0
                    last = j == job.G - 1 and kk == kc - 1
                    for t in range(2):
                        xh = xt_part(job, 0, kx)[:, t * P:(t + 1) * P]
                        xl = xt_part(job, 1, kx)[:, t * P:(t + 1) * P]
                        nc.tensor.matmul(a[t][:, 0:w], xh, hi, start=first, stop=False)
                        nc.tensor.matmul(a[t][:, 0:w], xh, lo, start=False, stop=False)
                        ins = nc.tensor.matmul(a[t][:, 0:w], xl, hi, start=False, stop=last)
                    if kk == kc - 1:
                        ins.then_inc(consumed, 1)
                    if job.name == "og":
                        gla_step(n, k)

            def bank(r, b):
                if not isinstance(r, int) or r > 0:
                    pe.wait_ge(tp_read[b], r)

            def transpose_round(r, src_of, per_bank=2):
                for b in range(2):
                    bank(r, b)
                    for f in range(per_bank):
                        for t in range(2):
                            ins = nc.tensor.transpose(tp[b][:, f * T + t * P:f * T + (t + 1) * P],
                                                      src_of(b * per_bank + f, t), ident[:, :])
                    ins.then_inc(tp_ready, 1)

            def transposes(job, n):
                name = job.name
                if name not in ("lr", "qk", "qk2", "pm", "wo", "f2o", "pg", "f1", "f2", "pool", "ub"):
                    return
                for t in range(2):
                    if name == "pg":
                        pe.wait_ge(hf_ready[t], n + 1)
                    elif name == "pm":
                        pe.wait_ge(merged_ready[t], n + 1)
                    else:
                        pe.wait_ge(evac[t], E(job, n))
                r = job.r0 + n
                if name == "lr":
                    for z in range(2):
                        bank(r, z)
                        for t in range(2):
                            ins = nc.tensor.transpose(tp[z][0:RANK, t * P:(t + 1) * P],
                                                      stage[:, t, z * RANK:(z + 1) * RANK], ident[:, :])
                        ins.then_inc(tp_ready, 1)
                elif name in ("qk", "qk2", "pm"):
                    transpose_round(r, lambda f, t: stage[:, t, f * P:(f + 1) * P])
                elif name in ("wo", "f2o", "pg"):
                    transpose_round(r, lambda f, t: H[:, t, n * NC + f * P:n * NC + (f + 1) * P])
                elif name in ("f1", "f2", "pool"):
                    transpose_round(r, lambda f, t: stage[:, t, f * P:(f + 1) * P], 1)
                elif name == "ub":
                    pe.wait_ge(loads["windows"], 16)
                    for b in range(2):
                        bank(r, b)
                        for f in range(2):
                            c = 4 * n + 2 * b + f
                            w = windows[:, c // 2, :]
                            nc.tensor.matmul(tp[b][:, f * T:(f + 1) * T], U[:, 0, c * P:(c + 1) * P],
                                             w[:, 0:T], start=True, stop=False, skip_group_check=True)
                            ins = nc.tensor.matmul(tp[b][:, f * T + P:(f + 1) * T], U[:, 1, c * P:(c + 1) * P],
                                                   w[:, T:T + P], start=False, stop=True, skip_group_check=True)
                        ins.then_inc(tp_ready, 1)

            def gk_piece(i):
                t, z, c = i // 4, (i // 2) % 2, i % 2
                if i == 0:
                    for b in range(2):
                        pe.wait_ge(tp_read[b], J["lr"].r0 + 1)
                    pe.wait_ge(loads["wgu"], 32)
                if i >= 2:
                    pe.wait_ge(gk_read, i - 1)
                nc.tensor.matmul(mx[i % 2][:, :], lrT[:, z, t * P:(t + 1) * P], wgu[:, z, cols(c)],
                                 start=True, stop=True).then_inc(gk_ready, 1)

            def gla_sums(h, u):
                d, lv = unit(u)
                n = h * UNITS + u
                if n == 0:
                    pe.wait_ge(sums_ready, 1)
                    pe.wait_ge(gk_read, 8)
                else:
                    pe.wait_ge(ex_ready, n)
                if u == 0:
                    pe.wait_ge(gsplit_lo, 2 * (h + 1))
                for c in range(2):
                    for t in range(2):
                        m = sums[:, 9 * d + (lv + 2 if lv >= 0 else t), :]
                        to = mx[0][:, c * T + t * P:c * T + (t + 1) * P]
                        nc.tensor.matmul(to, g_hi[:, t, d, c * P:(c + 1) * P], m, start=True, stop=False)
                        ins = nc.tensor.matmul(to, g_lo[:, t, d, c * P:(c + 1) * P], m, start=False, stop=True)
                ins.then_inc(e_ready, 1)

            def gla_diagonal(h):
                if h == 0:
                    for b in range(2):
                        pe.wait_ge(tp_read[b], J["qk"].r0 + 4)
                else:
                    pe.wait_ge(a_ready, h * (UNITS + 1))
                for t in range(2):
                    s = slice(t * P, (t + 1) * P)
                    for c in range(2):
                        ins = nc.tensor.matmul(mx[1][:, t * P:(t + 1) * P], qkT[:, 8 + 2 * h + c, s],
                                               qkT[:, 2 * h + c, s], start=(c == 0), stop=(c == 1))
                ins.then_inc(p_ready, 1)

            def gla_scores(h, u):
                d, lv = unit(u)
                n = h * UNITS + u
                pe.wait_ge(xq_ready, n + 1)
                pe.wait_ge(xk_ready, n + 1)
                pe.wait_ge(a_ready, h * (UNITS + 1) + u + 1)
                if lv < 0:
                    for c in range(2):
                        ins = nc.tensor.matmul(mx[1][:, 0:P], X[:, c, d * P:(d + 1) * P],
                                               X[:, c, (1 - d) * P:(2 - d) * P], start=(c == 0), stop=(c == 1))
                else:
                    for t in range(2):
                        s = slice(t * P, (t + 1) * P)
                        for c in range(2):
                            ins = nc.tensor.matmul(mx[1][:, t * P:(t + 1) * P], X[:, c, s], X[:, c, s],
                                                   start=(c == 0), stop=(c == 1))
                ins.then_inc(p_ready, 1)

            def gla_output(h):
                pe.wait_ge(a_ready, (h + 1) * (UNITS + 1))
                if h == 0:
                    for t in range(2):
                        pe.wait_ge(evac[t], E(J["v"], 3))
                for it in range(2):
                    bank(J["o"].r0 + h, it)
                    for jt in range(2):
                        ins = nc.tensor.matmul(tp[it][:, :], A_T[:, a_block(jt, it), :], V[:, jt, cols(h, GDV)],
                                               start=(jt == 0), stop=(jt == 1))
                    ins.then_inc(tp_ready, 1)

            def gla_step(h, k):
                if k == 0:
                    gla_diagonal(h)
                    gla_sums(h, 0)
                    return
                gla_scores(h, k - 1)
                gla_sums(h, k)
                if k == 15:
                    gla_scores(h, 15)
                    gla_output(h)

            def mlstm_scores(h):
                if h == 0:
                    pe.wait_ge(qk2_ready, 16)
                    pe.wait_ge(scan_ready, 1)
                else:
                    pe.wait_ge(pt_ready, h)
                nc.tensor.matmul(mx[1][:, 0:T], ident[0:MH, h:h + 1].broadcast_to([MH, P]), aR[:, :],
                                 start=True, stop=True)
                for st in range(2):
                    to = mx[0][:, 0:T] if st == 0 else mx[0][:, T:T + P]
                    for c in range(2):
                        ins = nc.tensor.matmul(to, qk2T[:, 16 + 2 * h + c, st * P:(st + 1) * P],
                                               qk2T[:, 2 * h + c, st * P:T], start=(c == 0), stop=(c == 1))
                ins.then_inc(s_ready, 1)

            def mlstm_output(h):
                r = J["num"].r0 + h
                pe.wait_ge(pt_ready, h + 1)
                if h == 0:
                    pe.wait_ge(ones_set, 2)
                for t in range(2):
                    pe.wait_ge(evac[t], E(J["v2"], h // 2))
                bank(r, 0)
                nc.tensor.matmul(tp[0][:, 0:MD + 1], PT[:, 0:P], VA[:, 0, h, 0:MD + 1],
                                 start=True, stop=True).then_inc(tp_ready, 1)
                bank(r, 1)
                nc.tensor.matmul(tp[1][:, 0:MD + 1], PT[:, P:T], VA[:, 0, h, 0:MD + 1], start=True, stop=False)
                nc.tensor.matmul(tp[1][:, 0:MD + 1], PT[:, T:T + P], VA[:, 1, h, 0:MD + 1],
                                 start=False, stop=True).then_inc(tp_ready, 1)

            def mlstm_gates():
                r = J["if"].r0
                pe.wait_ge(logf_ready, 1)
                for b, src in ((0, gi[:, :, 0:MH]), (1, logf[:, :, :])):
                    bank(r, b)
                    for t in range(2):
                        ins = nc.tensor.transpose(tp[b][0:MH, t * P:(t + 1) * P], src[:, t, :], ident[:, :])
                    ins.then_inc(tp_ready, 1)

            def mlstm_columns():
                r = J["if"].r0 + 1
                pe.wait_ge(em_ready, 1)
                for b, src in ((0, bR), (1, emR)):
                    bank(r, b)
                    for t in range(2):
                        ins = nc.tensor.transpose(tp[b][:, t * MH:(t + 1) * MH], src[:, t * P:(t + 1) * P],
                                                  ident[0:MH, 0:MH])
                    ins.then_inc(tp_ready, 1)

            def gla_transposes(h):
                for b in range(2):
                    pe.wait_ge(tp_read[b], J["o"].r0 + h + 1)
                transpose_round(J["y"].r0 + h, lambda f, t: H[:, t, h * NC + f * P:h * NC + (f + 1) * P])

            def after_granule(job, n, j, ns):
                name = job.name
                pj, pn = (job.prev, job.prev.n - 1 if job.prev else 0) if ns == 0 else (job, n - 1)
                if name == "qk" and n == 1:
                    gk_piece(j)
                if name == "oz" and j == 0:
                    mlstm_scores(n)
                if name == "oz" and j == 5:
                    mlstm_output(n)
                if name == "gb" and j == 4:
                    for t in range(2):
                        pe.wait_ge(ya_ready[t], n + 1)
                    transpose_round(J["ya"].r0 + n, lambda f, t: stage[:, t, f * P:(f + 1) * P])
                if name == "f2o" and n == 1 and j == 2:
                    pe.wait_ge(loads["p"], 16)
                    transpose_round(J["pt"].r0, lambda f, t: p_tok[:, t, f * P:(f + 1) * P], 1)
                if name == "qk2" and n == 0 and j == 4:
                    mlstm_gates()
                if name == "qk2" and n == 0 and j == 6:
                    mlstm_columns()
                if pj is not None and j == JT(job, pj.name):
                    transposes(pj, pn)

            pe.wait_ge(loads["ident"], 16)
            pe.wait_ge(loads["vec"], 160)
            nc.tensor.transpose(tp[0][:, 0:P], vec_raw[:, 0, :], ident[:, :])
            nc.tensor.transpose(tp[0][:, P:P + 32], vec_raw[0:32, 2, :], ident[0:32, 0:32]).then_inc(tp_ready, 1)
            nc.tensor.transpose(tp[1][:, 0:VEC_ROWS], vec_raw[0:VEC_ROWS, 1, :],
                                ident[0:VEC_ROWS, 0:VEC_ROWS]).then_inc(tp_ready, 1)
            pe.wait_ge(loads["x"], 16)
            for r in range(4):
                transpose_round(J["x"].r0 + r, lambda f, t: H[:, t, r * NC + f * P:r * NC + (f + 1) * P])

            for job in JOBS:
                def column_tile(n, ns):
                    for j in range(job.G):
                        if job.name == "wo" and n == 0 and j < GH:
                            gla_transposes(j)
                        product(job, n, j, ns)
                        after_granule(job, n, j, ns)
                if job.name in LOOPED:
                    column_tile(0, 0)
                    with pe.Fori(0, loop_passes(job)) as i:
                        for b in (1, 2):
                            column_tile(2 * i + b, b)
                    column_tile(job.n - 1, job.n - 1)
                else:
                    for n in range(job.n):
                        column_tile(n, n)

        @block.vector
        def _(dve):
            own_steps = [0]

            def settle(ins):
                own_steps[0] += 1
                ins.then_inc(dve_self, 1)
                dve.wait_ge(dve_self, own_steps[0])

            def split_lo(job, n, j, ns):
                g = gran(job, n, j)
                kc = job.gr[j][1]
                sg = job.g0 + ns * job.G + j
                slot, hl = sg % RAW_SLOTS, sg % HL_SLOTS
                dve.wait_ge(hi_ready, g + 1)
                nc.vector.tensor_tensor(w_lo[:, hl, 0:kc * job.w], raw[:, slot, 0:kc * job.w],
                                        w_hi[:, hl, 0:kc * job.w].bitcast(F32), ALU.subtract) \
                    .then_inc(lo_ready, 1)

            def xt_low(name, n, k_of, scale, full):
                hi, lo = DEST[name]
                for b in range(2):
                    dve.wait_ge(xt_hi, J[name].x0 + 2 * n + b + 1)
                    k = k_of(b)
                    if scale is None:
                        ins = nc.vector.tensor_tensor(
                            lo[:, bass.ds(k, full), :],
                            tp[b][:, 0:full * T].rearrange("p (k t) -> p k t", k=full),
                            hi[:, bass.ds(k, full), :].bitcast(F32), ALU.subtract)
                    else:
                        for f in range(full):
                            ins = nc.vector.scalar_tensor_tensor(
                                out=lo[:, k + f, :], in0=tp[b][:, f * T:(f + 1) * T], scalar=scale(k + f),
                                in1=hi[:, k + f, :].bitcast(F32), op0=ALU.mult, op1=ALU.subtract)
                    ins.then_inc(tp_read[b], 1)

            def mean_square(i, count):
                dve.wait_ge(squared, count)
                settle(nc.vector.tensor_reduce(msq[:, i, :], ssq[:, i, :, :], AX.X, ALU.add))
                nc.vector.tensor_scalar(msq[:, i, :], msq[:, i, :], 1.0 / D, EPS, ALU.mult, ALU.add) \
                    .then_inc(ms_ready, 1)

            def evacuate(job, n, ns):
                name = job.name
                a = acc_of(job, ns)
                if name in ("og", "zb", "gb", "ga"):
                    return
                dve.wait_ge(consumed, done(job, n))
                if name in ("lr", "qk", "v", "qk2", "v2", "ub", "pp"):
                    w = job.w
                    scale = None if name == "pp" else rstd[:, 0 if name in ("lr", "qk", "v") else S2, 1:2]
                    dst = {"lr": stage, "qk": stage, "qk2": stage, "v": V, "v2": VA, "ub": U, "pp": PPJ}[name]
                    src = a[1][:, 0:w]
                    if name == "lr":
                        dve.wait_ge(rstd_ready, 1)
                    if name in ("qk", "qk2"):
                        dve.wait_ge(tp_ready, 2 * (job.r0 + n))
                    if name == "v":
                        dve.wait_ge(g_ready, 8)
                    if name == "ub":
                        dve.wait_ge(s2_ready, 1)
                    if name == "v2":
                        dst, src = dst[:, 1, 2 * n:2 * n + 2, 0:MD], src.rearrange("p (h d) -> p h d", h=2)
                    elif dst is stage:
                        dst = dst[:, 1, 0:w]
                    else:
                        dst = dst[:, 1, cols(n)]
                    if scale is None:
                        nc.vector.tensor_copy(dst, src).then_inc(evac[1], 1)
                    else:
                        nc.vector.tensor_scalar(dst, src, scale, None, ALU.mult).then_inc(evac[1], 1)
                elif name in ("wo", "f1o", "f2o"):
                    if name == "wo":
                        dve.wait_ge(loads["xagain"], 16)
                    old = xagain if name == "wo" else H
                    for t in range(2):
                        nc.vector.tensor_tensor(H[:, t, cols(n)], a[t][:, :], old[:, t, cols(n)], ALU.add) \
                            .then_inc(evac[t], 1)
                elif name in ("f1", "f2"):
                    dve.wait_ge(tp_ready, 2 * (job.r0 + n))
                    for t in range(2):
                        dve.wait_ge(f_gate, 2 * n + (0 if name == "f1" else 2 * J["f1"].n) + t + 1)
                        nc.vector.scalar_tensor_tensor(
                            out=stage[:, t, 0:HF], in0=a[t][:, HF:2 * HF], scalar=rstd[:, 1, t:t + 1],
                            in1=gates[:, t, 0:HF], op0=ALU.mult, op1=ALU.mult).then_inc(evac[t], 1)
                elif name == "pool":
                    for t in range(2):
                        dve.wait_ge(evac[t], E(J["zb"], 1))
                    dve.wait_ge(tp_ready, 2 * (job.r0 + n))
                    for t in range(2):
                        nc.vector.tensor_tensor(stage[:, t, 0:256], a[t][:, 0:256], ZB[:, t, cols(n, 256)],
                                                ALU.mult).then_inc(evac[t], 1)
                elif name == "if":
                    dve.wait_ge(loads["gbias"], 32)
                    for t in range(2):
                        nc.vector.scalar_tensor_tensor(
                            out=gi[:, t, :], in0=a[t][:, 0:2 * MH], scalar=rstd[:, S2, t:t + 1],
                            in1=gate_bias[:, :], op0=ALU.mult, op1=ALU.add).then_inc(evac[t], 1)
                elif name == "oz":
                    for t in range(2):
                        dve.wait_ge(oz_sg, 2 * n + t + 1)
                        nc.vector.tensor_tensor(gates[:, t, 0:MD], gates[:, t, 0:MD], gates[:, t, MD:2 * MD],
                                                ALU.mult).then_inc(oz_prod, 1)
                    for t in range(2):
                        dve.wait_ge(oz_prod, 2 * n + t + 1)
                        nc.vector.scalar_tensor_tensor(
                            out=GB[:, t, cols(n, MD)], in0=a[t][:, MD:2 * MD], scalar=rstd[:, S2, t:t + 1],
                            in1=gates[:, t, 0:MD], op0=ALU.mult, op1=ALU.mult).then_inc(evac[t], 1)
                elif name == "pb":
                    for t in range(2):
                        dve.wait_ge(evac[t], E(J["gb"], n))
                        nc.vector.tensor_tensor(GB[:, t, cols(n)], a[t][:, :], GB[:, t, cols(n)], ALU.mult) \
                            .then_inc(evac[t], 1)
                elif name == "pm":
                    for t in range(2):
                        nc.vector.tensor_tensor(GA[:, t, cols(n)], a[t][:, :], GA[:, t, cols(n)], ALU.mult) \
                            .then_inc(evac[t], 1)
                    dve.wait_ge(tp_ready, 2 * (job.r0 + n))
                    for t in range(2):
                        dve.wait_ge(evac[t], E(job, n))
                        nc.vector.tensor_tensor(stage[:, t, :], GA[:, t, cols(n)], GB[:, t, cols(n)], ALU.add) \
                            .then_inc(merged_ready[t], 1)
                elif name == "out":
                    dve.wait_ge(loads["npw"], 16)
                    for t in range(2):
                        dve.wait_ge(squared, SQ["out"] + 2 * n + t + 1)
                        nc.vector.tensor_tensor(OUT[:, t, cols(n)], a[t][:, :], npw_bc[:, cols(n)], ALU.mult) \
                            .then_inc(evac[t], 1)

            def evacuate_transposed(job, n):
                name = job.name
                if name == "lr":
                    dve.wait_ge(tp_ready, 2 * job.r0 + 2)
                    dve.wait_ge(ones_row_set, 1)
                    nc.vector.tensor_copy(lrT[0:RANK, 1, :], tp[1][0:RANK, 0:T]).then_inc(tp_read[1], 1)
                elif name == "qk":
                    dve.wait_ge(tp_ready, 2 * (job.r0 + n) + 2)
                    nc.vector.tensor_scalar(qkT[:, 4 * n + 2:4 * n + 4, :],
                                            tp[1][:, :].rearrange("p (k t) -> p k t", k=2),
                                            GDK ** -0.5 if n < 2 else 1.0, None, ALU.mult) \
                        .then_inc(tp_read[1], 1)
                elif name in ("wo", "f2o", "pg"):
                    xt_low(name, n, lambda b: 4 * n + 2 * b, lambda k: vcol(NORM_OF[name], k), 2)
                elif name in ("ub", "pm"):
                    xt_low(name, n, lambda b: 4 * n + 2 * b, None, 2)
                elif name in ("f1", "f2"):
                    xt_low(name, n, lambda b: 2 * n + b, None, 1)
                elif name == "pool":
                    xt_low(name, n, lambda b: 2 * n + b, lambda k: vcol("pool_scale", k), 1)

            def convolve(n, b):
                job = J["qk2"]
                dve.wait_ge(tp_ready, 2 * (job.r0 + n) + b + 1)
                if n:
                    dve.wait_ge(qk2_ready, 2 * n)
                for tap in range(3, -1, -1):
                    s = 3 - tap
                    for f in range(2):
                        k = 4 * n + 2 * b + f
                        w = cw[:, tap * 32 + k:tap * 32 + k + 1]
                        src = tp[b][:, f * T:(f + 1) * T - s]
                        dst = conv[:, 2 * b + f, s:T]
                        if tap == 3:
                            ins = nc.vector.tensor_scalar(dst, src, w, cbias[:, k:k + 1], ALU.mult, ALU.add)
                        else:
                            ins = nc.vector.scalar_tensor_tensor(out=dst, in0=src, scalar=w, in1=dst,
                                                                 op0=ALU.mult, op1=ALU.add)
                    if tap:
                        settle(ins)
                ins.then_inc(tp_read[b], 1)

            def gk_read_of(i):
                t, z, c = i // 4, (i // 2) % 2, i % 2
                dve.wait_ge(gk_ready, i + 1)
                if i == 0:
                    dve.wait_ge(sums_ready, 1)
                    dve.wait_ge(masks_ready, 2)
                low = V[:, t, z * GK + c * NC:z * GK + (c + 1) * NC]
                nc.vector.tensor_scalar(low, mx[i % 2][:, :], 0.0, None, ALU.min).then_inc(gk_min, 1)
                dve.wait_ge(gk_min, i + 1)
                nc.vector.scalar_tensor_tensor(out=G[:, t, z, cols(c)], in0=low, scalar=2.0,
                                               in1=mx[i % 2][:, :], op0=ALU.mult, op1=ALU.subtract) \
                    .then_inc(gk_read, 1)

            def gk_decay(i):
                t, z, c = i // 4, (i // 2) % 2, i % 2
                dve.wait_ge(gk_ln, i + 1)
                nc.vector.tensor_tensor(G[:, t, z, cols(c)], V[:, t, z * GK + c * NC:z * GK + (c + 1) * NC],
                                        G[:, t, z, cols(c)], ALU.subtract).then_inc(g_ready, 1)

            def gla_split(h):
                for t in range(2):
                    dve.wait_ge(gsplit_hi, 2 * h + t + 1)
                    nc.vector.tensor_tensor(g_lo[:, t, :, :], G[:, t, :, h * GDK:(h + 1) * GDK],
                                            g_hi[:, t, :, :].bitcast(F32), ALU.subtract).then_inc(gsplit_lo, 1)
                dve.wait_ge(p_ready, h * (UNITS + 1) + 1)
                if h == 0:
                    dve.wait_ge(loads["diag"], 16)
                else:
                    dve.wait_ge(tp_ready, 2 * (J["o"].r0 + h))
                nc.vector.tensor_tensor(A_T[:, 0:2, :], mx[1][:, 0:2 * P].rearrange("p (t i) -> p t i", t=2),
                                        diag2[:, :].rearrange("p (t i) -> p t i", t=2), ALU.mult) \
                    .then_inc(a_ready, 1)

            def gla_unit(h, u):
                d, lv = unit(u)
                q_half, _, l = unit_rows(u)
                n = h * UNITS + u
                dve.wait_ge(ex_ready, n + 1)
                if u:
                    dve.wait_ge(p_ready, h * (UNITS + 1) + u + 1)
                nc.vector.tensor_tensor(halves(X[:, :, :], q_half, l), halves(qkT[:, 2 * h:2 * h + 2, :], q_half, l),
                                        halves(Ex[:, :, :], q_half, l), ALU.mult).then_inc(xq_ready, 1)
                dve.wait_ge(p_ready, h * (UNITS + 1) + u + 2)
                dve.wait_ge(a_ready, h * (UNITS + 1) + u + 1)
                if lv < 0:
                    nc.vector.tensor_copy(A_T[:, a_block(d, 1 - d), :], mx[1][:, 0:P]).then_inc(a_ready, 1)
                else:
                    nc.vector.copy_predicated(
                        A_T[:, 0:2, :].rearrange("p t i -> p (t i)"), masks[:, d * len(LEVELS) + lv, :],
                        mx[1][:, 0:2 * P]).then_inc(a_ready, 1)

            def gla_mean(h):
                dve.wait_ge(squared, SQ["gla"] + 2 * (h + 1))
                nc.vector.tensor_scalar(hms[:, 2 * h:2 * h + 2], hss[:, 2 * h:2 * h + 2], 1.0 / GDV, EPS,
                                        ALU.mult, ALU.add).then_inc(ho_ms, 1)

            def gla_gate(h):
                dve.wait_ge(ho_rstd, h + 1)
                for t in range(2):
                    dve.wait_ge(evac[t], E(J["og"], h))
                    nc.vector.scalar_tensor_tensor(
                        out=H[:, t, cols(h)], in0=tp[t][:, :], scalar=hrs[:, 2 * h + t:2 * h + t + 1],
                        in1=H[:, t, cols(h)], op0=ALU.mult, op1=ALU.mult).then_inc(tp_read[t], 1)

            def mlstm_weights(h):
                dve.wait_ge(s_ready, h + 1)
                if h:
                    dve.wait_ge(pt_ready, h)
                settle(nc.vector.tensor_scalar(W[:, 0:T], mx[1][:, 0:T], bT[:, 0, h:h + 1], 0.0, ALU.add, ALU.min))
                nc.vector.tensor_scalar(W[:, T:T + P], mx[1][:, P:T], bT[:, 1, h:h + 1], 0.0, ALU.add, ALU.min) \
                    .then_inc(w_ready, 1)

            def mlstm_probs(h):
                dve.wait_ge(wmask_ready, 2 * (h + 1))
                if h:
                    dve.wait_ge(tp_ready, 2 * (J["num"].r0 + h))
                nc.vector.scalar_tensor_tensor(out=PT[:, :], in0=mx[0][:, 0:T + P], scalar=MD ** -0.5,
                                               in1=W[:, :], op0=ALU.mult, op1=ALU.mult).then_inc(pt_ready, 1)

            def mlstm_divide(h):
                r = J["num"].r0 + h
                dve.wait_ge(tp_ready, 2 * r + 2)
                for t in range(2):
                    ins = nc.vector.scalar_tensor_tensor(
                        out=den[:, t:t + 1], in0=tp[t][:, MD:MD + 1], scalar=-1.0, in1=emT[:, t, h:h + 1],
                        op0=ALU.mult, op1=ALU.max)
                settle(ins)
                for t in range(2):
                    ins = nc.vector.tensor_tensor(den[:, t:t + 1], tp[t][:, MD:MD + 1], den[:, t:t + 1], ALU.max)
                settle(ins)
                settle(nc.vector.reciprocal(rden[:, :], den[:, :]))
                for t in range(2):
                    nc.vector.tensor_scalar(VA[:, t, h, 0:MD], tp[t][:, 0:MD], rden[:, t:t + 1], None,
                                            ALU.mult).then_inc(tp_read[t], 1)

            def mlstm_gated(n):
                dve.wait_ge(ho_rstd, GH + 1)
                dve.wait_ge(tp_ready, 2 * (J["ya"].r0 + n))
                for t in range(2):
                    dve.wait_ge(evac[t], E(J["oz"], 2 * n + 1))
                    for h in (2 * n, 2 * n + 1):
                        ins = nc.vector.scalar_tensor_tensor(
                            out=stage[:, t, (h % 2) * MD:(h % 2 + 1) * MD], in0=VA[:, t, h, 0:MD],
                            scalar=hrs[:, 2 * h + t:2 * h + t + 1], in1=GB[:, t, cols(h, MD)],
                            op0=ALU.mult, op1=ALU.mult)
                    ins.then_inc(ya_ready[t], 1)

            def mlstm_forget():
                for t in range(2):
                    dve.wait_ge(evac[t], E(J["if"], 0))
                nc.vector.scalar_tensor_tensor(out=minus_abs_f[:, :, :], in0=gi[:, :, MH:2 * MH], scalar=-1.0,
                                               in1=gi[:, :, MH:2 * MH], op0=ALU.mult, op1=ALU.min) \
                    .then_inc(abs_ready, 1)
                dve.wait_ge(ln_ready, 1)
                nc.vector.scalar_tensor_tensor(out=logf[:, :, :], in0=gi[:, :, MH:2 * MH], scalar=0.0,
                                               in1=lnf[:, :, :], op0=ALU.min, op1=ALU.subtract) \
                    .then_inc(logf_ready, 1)

            def mlstm_scans():
                r = J["if"].r0
                dve.wait_ge(tp_ready, 2 * r + 2)
                dve.wait_ge(ones_set, 2)
                settle(nc.vector.tensor_copy(iR[:, :], tp[0][0:MH, 0:T]))
                nc.vector.tensor_copy(fR[:, :], tp[1][0:MH, 0:T]).then_inc(tp_read[1], 1)
                dve.wait_ge(tp_read[1], r + 1)
                settle(nc.vector.tensor_tensor_scan(Fc[:, :], ones8[:, :], fR[:, :], 0.0, ALU.mult, ALU.add))
                settle(nc.vector.tensor_tensor_scan(mR[:, :], fR[:, :], iR[:, :], 0.0, ALU.add, ALU.max))
                nc.vector.tensor_tensor(bR[:, :], iR[:, :], Fc[:, :], ALU.subtract).then_inc(tp_read[0], 1)
                nc.vector.tensor_tensor(aR[:, :], Fc[:, :], mR[:, :], ALU.subtract).then_inc(scan_ready, 1)

            def mlstm_columns():
                r = J["if"].r0 + 1
                dve.wait_ge(tp_ready, 2 * r + 2)
                nc.vector.tensor_copy(bT[:, :, :], tp[0][:, 0:2 * MH].rearrange("p (t h) -> p t h", t=2)) \
                    .then_inc(tp_read[0], 1)
                nc.vector.tensor_copy(emT[:, :, :], tp[1][:, 0:2 * MH].rearrange("p (t h) -> p t h", t=2)) \
                    .then_inc(tp_read[1], 1)

            def second_norms():
                mean_square(3, SQ["pg"] + 16)
                settle(nc.vector.tensor_reduce(msq[:, 4, :], ssq[:, 4, :, :], AX.X, ALU.add))
                dve.wait_ge(rstd_ready, 4)
                settle(nc.vector.tensor_tensor(msq[:, 4, :], msq[:, 4, :], rstd[:, 3, :], ALU.mult))
                settle(nc.vector.tensor_tensor(msq[:, 4, :], msq[:, 4, :], rstd[:, 3, :], ALU.mult))
                nc.vector.tensor_scalar(msq[:, 4, :], msq[:, 4, :], 1.0 / D, EPS, ALU.mult, ALU.add) \
                    .then_inc(ms_ready, 1)
                dve.wait_ge(rstd_ready, 5)
                nc.vector.tensor_tensor(rstd[:, S2, :], rstd[:, 3, :], rstd[:, 4, :], ALU.mult) \
                    .then_inc(s2_ready, 1)

            def after_split(job, n, j, ns):
                name = job.name
                pj, pn, pns = (job.prev, job.prev.n - 1 if job.prev else 0, job.prev.n - 1 if job.prev else 0) \
                    if ns == 0 else (job, n - 1, ns - 1)
                if name == "qk" and n == 1 and j >= LAG:
                    gk_read_of(j - LAG)
                if name == "qk" and n == 2 and j < LAG:
                    gk_read_of(j - LAG + 8)
                if name == "v" and n == 0:
                    gk_decay(j)
                if name == "og" and j >= LAG:
                    if j == LAG:
                        gla_split(n)
                    gla_unit(n, 2 * (j - LAG))
                    gla_unit(n, 2 * (j - LAG) + 1)
                if (name == "og" and n >= 1 or name == "wo" and n == 0) and j < LAG:
                    h = n - 1 if name == "og" else GH - 1
                    gla_unit(h, 2 * (j - LAG + 8))
                    gla_unit(h, 2 * (j - LAG + 8) + 1)
                    if j == LAG - 1:
                        gla_mean(h)
                if name == "oz" and n >= 1 and j == 1:
                    mlstm_divide(n - 1)
                if name == "oz" and j == 4:
                    mlstm_weights(n)
                if name == "oz" and j == 5:
                    mlstm_probs(n)
                if name == "gb" and n == 0 and j == 1:
                    mlstm_divide(MH - 1)
                if pj is not None and j == JE(job):
                    evacuate(pj, pn, pns)
                if pj is not None and pj.name == "pg" and j == 4:
                    dve.wait_ge(sgp_ready, pn + 1)
                    for t in range(2):
                        nc.vector.tensor_tensor(H[:, t, cols(pn)], H[:, t, cols(pn)], gates[:, t, :], ALU.add) \
                            .then_inc(h_ready, 1)
                if pj is not None and pj.name == "pg" and j == 5:
                    dve.wait_ge(loads["fn"], 16)
                    for t in range(2):
                        dve.wait_ge(squared, SQ["pg"] + 4 * pn + t + 1)
                        nc.vector.tensor_tensor(H[:, t, cols(pn)], H[:, t, cols(pn)], fn_bc[:, cols(pn)],
                                                ALU.mult).then_inc(hf_ready[t], 1)
                if name == "f2o" and n == 1 and j == JV(job, "") - 1:
                    xt_low("pt", 0, lambda b: b, None, 1)
                if pj is not None and j == JV(job, pj.name):
                    evacuate_transposed(pj, pn)
                if pj is not None and pj.name == "qk2" and j in (6, 7):
                    convolve(pn, j - 6)
                if (name == "og" and n >= 1) and j == LAG:
                    gla_gate(n - 1)
                if name == "wo" and n == 0 and j == LAG:
                    gla_gate(GH - 1)
                if name == "wo" and n == 0 and j in (3, 4, 5):
                    for h in {3: (0, 1), 4: (2,), 5: (3,)}[j]:
                        xt_low("y", h, lambda b: 4 * h + 2 * b, lambda k: vcol("gla_out_norm", k % 4), 2)
                if name == "gb" and n == 0 and j == 4:
                    dve.wait_ge(squared, SQ["mlstm"] + 2 * MH)
                    nc.vector.tensor_scalar(hms[:, :], hss[:, :], 1.0 / MD, EPS, ALU.mult, ALU.add) \
                        .then_inc(ho_ms, 1)
                if name == "gb" and j == 4:
                    mlstm_gated(n)
                if name == "gb" and j == 7:
                    xt_low("ya", n, lambda b: 4 * n + 2 * b, lambda k: vcol("mlstm_norm", k), 2)
                if name == "qk2" and n == 0 and j == 4:
                    mlstm_forget()
                if name == "qk2" and n == 0 and j == 5:
                    mlstm_scans()
                if name == "qk2" and n == 0 and j == 7:
                    mlstm_columns()
                if name == "f1" and ns == 0 and j == 4:
                    mean_square(1, SQ["wo"] + 8)
                if name == "pp" and n == 1:
                    mean_square(2, SQ["f2o"] + 8)
                if name == "ub" and n == 0 and j == 7:
                    second_norms()

            dve.wait_ge(tp_ready, 2)
            nc.vector.tensor_copy(vec[:, :], tp[1][:, 0:VEC_ROWS]).then_inc(tp_read[1], 1)
            settle(nc.vector.tensor_copy(cbias[:, :], tp[0][:, P:P + 32]))
            nc.vector.tensor_copy(cw[:, :], tp[0][:, 0:P]).then_inc(tp_read[0], 1)
            dve.wait_ge(tp_read[1], 1)
            for r in range(4):
                xt_low("x", r, lambda b: 4 * r + 2 * b, lambda k: vcol("mixer_norm", k), 2)
                if r == 1:
                    for j in range(HL_SLOTS):
                        split_lo(J["lr"], 0, j, 0)
            mean_square(0, SQ["x"] + 8)

            for job in JOBS:
                def column_tile(n, ns):
                    for j in range(job.G):
                        if not (job.name == "lr" and j < HL_SLOTS):
                            split_lo(job, n, j, ns)
                        after_split(job, n, j, ns)
                if job.name in LOOPED:
                    column_tile(0, 0)
                    with dve.Fori(0, loop_passes(job)) as i:
                        for b in (1, 2):
                            column_tile(2 * i + b, b)
                    column_tile(job.n - 1, job.n - 1)
                else:
                    for n in range(job.n):
                        column_tile(n, n)
            evacuate(J["out"], 3, 3)
            mean_square(5, SQ["out"] + 8)
            dve.wait_ge(rstd_ready, 6)
            dve.wait_ge(x2_ready, 2)
            for n in range(4):
                for t in range(2):
                    dve.wait_ge(evac[t], E(J["out"], n))
                    nc.vector.scalar_tensor_tensor(
                        out=OUT[:, t, cols(n)], in0=OUT[:, t, cols(n)], scalar=rstd[:, 5, t:t + 1],
                        in1=H[:, t, cols(n)], op0=ALU.mult, op1=ALU.add).then_inc(y_ready, 1)


def constants():
    import numpy as np

    s, r = np.arange(P)[:, None], np.arange(P)[None, :]
    sums = np.zeros((P, 18, P), np.float32)
    masks = np.zeros((P, 14, P), np.float32)
    for d in range(2):
        if d == 0:
            sums[:, 0] = s > r
            sums[:, 1] = s <= r
        else:
            sums[:, 9] = s >= r
            sums[:, 10] = s < r
        for i, l in enumerate(LEVELS):
            same = s // (2 * l) == r // (2 * l)
            s_up, r_up = (s // l) % 2 == 1, (r // l) % 2 == 1
            if d == 0:
                keep = (r_up & s_up & (s <= r)) | (~r_up & ~s_up & (s > r))
                pair = same & ~s_up & r_up
            else:
                keep = (~r_up & ~s_up & (s >= r)) | (r_up & s_up & (s < r))
                pair = same & s_up & ~r_up
            sums[:, 9 * d + 2 + i] = keep & same
            masks[:, 7 * d + i, :] = pair
    diag = np.tile(2.0 * np.eye(P, dtype=np.float32), (1, 2))
    t = np.arange(T)
    windows = np.zeros((T, 4, T), np.float64)
    for g, w in enumerate(POOL_WINDOWS):
        low = np.maximum(t + 1 - w, 0)
        inside = (t[:, None] >= low[None, :]) & (t[:, None] <= t[None, :])
        windows[:, g] = inside / (t + 1 - low)[None, :] - np.eye(T)
    packed = np.concatenate([windows[0:P], windows[P:T, :, P:T]], axis=2)
    return {
        "c_ident": np.eye(P, dtype=np.float32), "c_sums": sums.reshape(P, -1),
        "c_masks": masks.reshape(P, -1), "c_diag": diag,
        "c_windows": packed.reshape(P, -1).astype(np.float32),
    }


_INS = ["x", "p", "mixer_norm", "gla_w_in", "gla_w_gate_up", "gla_b_gate", "gla_out_norm", "gla_w_out",
        "ffn_norm", "ffn_w_in", "ffn_w_out", "ple_norm", "ple_w_gate", "ple_w_proj", "final_norm",
        "norm_pre_w_2", "w_in_2", "mlstm_i_bias_2", "mlstm_f_bias_2", "qk_conv_w_2", "qk_conv_b_2",
        "mlstm_norm_w_2", "pool_w_2", "pool_scale_2", "w_proj_mlstm_2", "w_proj_pool_2", "w_out_2",
        "norm_post_w_2"]
_MATRICES = ("gla_w_in", "gla_w_out", "ffn_w_in", "ffn_w_out", "ple_w_gate", "ple_w_proj", "w_in_2",
             "w_proj_mlstm_2", "w_proj_pool_2", "w_out_2")


def kernel(**inputs):
    import numpy as np
    import concourse.bacc as bacc
    from concourse.bass_utils import run_bass_kernel_spmd

    nc = bacc.Bacc("TRN2", target_bir_lowering=False, num_devices=1)
    arrays, args = {}, []
    for name in _INS:
        a = np.ascontiguousarray(inputs[name])
        if name in _MATRICES:
            a = a.reshape(a.shape[1:])
        arrays["in_" + name] = a
    for name, a in constants().items():
        arrays["in_" + name] = a
    for name, a in arrays.items():
        args.append(nc.dram_tensor(name, a.shape, mybir.dt.from_np(a.dtype), kind="ExternalInput").ap())
    args.append(nc.dram_tensor("out_y", (1, T, D), F32, kind="ExternalOutput").ap())
    build(nc, *args)
    r = run_bass_kernel_spmd(nc, [arrays], core_ids=[0])
    return r.results[0]["out_y"]
```

```python
from contextlib import ExitStack

import concourse.bass as bass
from concourse import mybir

F32 = mybir.dt.float32
F32R = mybir.dt.float32r
BF16 = mybir.dt.bfloat16
I8 = mybir.dt.int8
ACT = mybir.ActivationFunctionType
ALU = mybir.AluOpType
AX = mybir.AxisListType

P = 128
T = 256
D = 2048
EPS = 1e-6
DFF = 5632
HF = 256
NC = 512
RAW_SLOTS = 8
HL_SLOTS = 4
LAG = 3

GH, GDK, GDV = 4, 256, 512
GK = GH * GDK
RANK = 16
GATE_NORM = 16.0
LEVELS = [64, 32, 16, 8, 4, 2, 1]
SCORES = 1 + len(LEVELS)
UNITS = 2 * SCORES

MH, MD = 8, 256
VW = 258
POOL_WINDOWS = (2, 4, 8, 16)

VEC = {}
_at = 0
for _name, _rows in (("mixer_norm", 16), ("gla_out_norm", 4), ("ffn_norm", 16), ("ple_norm", 16),
                     ("final_norm", 16), ("norm_pre", 16), ("pool_scale", 8), ("mlstm_norm", 16)):
    VEC[_name] = (_at, _rows)
    _at += _rows
VEC_ROWS = _at


class Job:

    def __init__(self, name, n, granules, width=NC, per_granule=1):
        self.name, self.n, self.gr, self.w, self.dmas = name, n, granules, width, per_granule
        self.G = len(granules)


def granules(k_tiles, size=2):
    return [(k, min(size, k_tiles - k)) for k in range(0, k_tiles, size)]


def plan():
    full = granules(16)
    jobs = [
        Job("lr", 1, full, 2 * RANK), Job("qk", 4, full), Job("v", 4, full), Job("og", 4, full),
        Job("wo", 4, full),
        Job("f1", 12, full, NC, 2), Job("f1o", 4, granules(24)),
        Job("f2", 10, full, NC, 2), Job("f2o", 4, granules(20)),
        Job("pp", 4, granules(2)), Job("pg", 4, full),
        Job("ub", 2, full), Job("zb", 2, full), Job("pool", 4, granules(2, 1), 256),
        Job("if", 1, full, 2 * MH), Job("qk2", 8, full), Job("v2", 4, full),
        Job("oz", 8, full, NC, 2), Job("gb", 4, full), Job("ga", 4, full),
        Job("pb", 4, granules(8)), Job("pm", 4, full), Job("out", 4, full),
    ]
    tile = gran = 0
    landed = [0] * RAW_SLOTS
    for prev, job in zip([None] + jobs[:-1], jobs):
        job.prev, job.t0, job.g0, job.landed0 = prev, tile, gran, list(landed)
        tile += job.n
        for q in range(job.n * job.G):
            landed[(gran + q) % RAW_SLOTS] += 16 * job.dmas
        gran += job.n * job.G
    byname = {j.name: j for j in jobs}
    r = x = 0
    for name, n, split in (
            ("vec", 1, 0), ("x", 4, 1), ("lr0", 1, 0), ("lr", 1, 0), ("qk", 4, 0), ("o", 4, 0), ("y", 4, 1),
            ("wo", 4, 1), ("f1", 12, 1), ("f2", 10, 1), ("pt", 1, 1), ("f2o", 4, 1), ("pg", 4, 1),
            ("ub", 2, 1), ("pool", 4, 1), ("if0", 1, 0), ("if", 2, 0), ("qk2", 8, 0), ("num", 8, 0), ("ya", 4, 1),
            ("pm", 4, 1)):
        if name not in byname:
            byname[name] = Job(name, n, [])
        byname[name].r0, byname[name].x0 = r, x
        r, x = r + n, x + 2 * n * split
    return jobs, byname


def build(nc, x, p, mixer_norm, gla_w_in, gla_w_gate_up, gla_b_gate, gla_out_norm, gla_w_out,
          ffn_norm, ffn_w_in, ffn_w_out, ple_norm, ple_w_gate, ple_w_proj, final_norm,
          norm_pre, w_in2, i_bias, f_bias, conv_w, conv_b, mlstm_norm, pool_w, pool_scale,
          w_mlstm, w_pool, w_out2, norm_post,
          c_ident, c_sums, c_masks, c_diag, c_windows, out):
    JOBS, J = plan()

    def rows(ap):
        return ap.rearrange("(k p) n -> p k n", p=P)

    gin, win = rows(gla_w_in), rows(w_in2)
    fin, fout = rows(ffn_w_in), rows(ffn_w_out)
    qkv_at = 5 * D + 2 * MH
    SRC = {
        "lr": (gin, lambda n: 2 * GK + 2 * D), "qk": (gin, lambda n: n * NC),
        "v": (gin, lambda n: 2 * GK + n * NC), "og": (gin, lambda n: 2 * GK + D + n * NC),
        "wo": (rows(gla_w_out), lambda n: n * NC),
        "f1": (fin, lambda n: n * HF), "f1o": (fout[:, 0:24, :], lambda n: n * NC),
        "f2": (fin, lambda n: (n + 12) * HF), "f2o": (fout[:, 24:44, :], lambda n: n * NC),
        "pp": (rows(ple_w_proj), lambda n: n * NC), "pg": (rows(ple_w_gate), lambda n: n * NC),
        "ub": (win, lambda n: qkv_at + n * NC), "zb": (win, lambda n: qkv_at + 1024 + n * NC),
        "pool": None,
        "if": (win, lambda n: 5 * D), "qk2": (win, lambda n: n * NC),
        "v2": (win, lambda n: 2 * D + n * NC), "oz": (win, lambda n: 3 * D + n * MD),
        "gb": (win, lambda n: qkv_at + 2048 + D + n * NC), "ga": (win, lambda n: qkv_at + 2048 + n * NC),
        "pb": (rows(w_pool), lambda n: n * NC), "pm": (rows(w_mlstm), lambda n: n * NC),
        "out": (rows(w_out2), lambda n: n * NC),
    }
    SECOND_HALF = {"f1": DFF, "f2": DFF, "oz": D}

    ctx = ExitStack()
    with ctx:
        base = (nc.sbuf_base + 63) // 64 * 64
        used_to = [base]

        def at(name, shape, dt, offset):
            return nc.alloc_sbuf_tensor_at(name, shape, dt, offset=offset)

        def own(name, shape, dt, size):
            offset = used_to[0]
            used_to[0] += (size + 31) // 32 * 32
            return at(name, shape, dt, offset), offset

        raw, _ = own("raw", [P, RAW_SLOTS, 2 * NC], F32, RAW_SLOTS * 4096)
        w_hi, _ = own("w_hi", [P, HL_SLOTS, 2 * NC], F32R, HL_SLOTS * 4096)
        w_lo, _ = own("w_lo", [P, HL_SLOTS, 2 * NC], F32R, HL_SLOTS * 4096)
        xa_hi, xa_at = own("xa_hi", [P, 16, T], F32R, 16384)
        xa_lo, _ = own("xa_lo", [P, 16, T], F32R, 16384)
        xb_hi, xb_at = own("xb_hi", [P, 16, T], F32R, 16384)
        xb_lo, _ = own("xb_lo", [P, 16, T], F32R, 16384)
        H, h_at = own("H", [P, 2, D], F32, 16384)
        ident, _ = own("ident", [P, P], F32, 512)
        vec, _ = own("vec", [P, VEC_ROWS], F32, 4 * VEC_ROWS)
        cbias, _ = own("cbias", [P, 32], F32, 128)
        cw, _ = own("cw", [P, P], F32, 512)
        ssq, _ = own("ssq", [P, 6, 2, 4], F32, 192)
        msq, _ = own("msq", [P, 8, 2], F32, 64)
        rstd, _ = own("rstd", [P, 8, 2], F32, 64)
        S2 = 6
        half, _ = own("half", [P, 16], F32, 64)
        hss, _ = own("hss", [P, 16], F32, 64)
        hms, _ = own("hms", [P, 16], F32, 64)
        hrs, _ = own("hrs", [P, 16], F32, 64)
        junk, _ = own("junk", [P, NC], BF16, 1024)
        ov = used_to[0]
        room = nc.sbuf_usable_end - ov

        V = at("V", [P, 2, D], F32, xb_at)
        G = at("G", [P, 2, 2, GK], F32, xb_at + 16384)
        masks_raw = at("masks_raw", [P, 7, P], F32, xb_at + 16384)
        vec_raw = at("vec_raw", [P, 3, P], F32, xb_at + 12288)
        o = ov
        stage = at("stage", [P, 2, NC], F32, o); o += 4096
        gates_at = o
        gates = at("gates", [P, 2, NC], F32, o); o += 4096
        phase = o
        qkT = at("qkT", [P, 16, T], F32, o); o += 16384
        A_T = at("A_T", [P, 2, 4, P], F32, o); o += 4096
        Ex = at("Ex", [P, 2, T], F32, o); o += 2048
        X = at("X", [P, 2, 2, 2, T], F32, o); o += 8192
        sums = at("sums", [P, 18, P], F32, o); o += 18 * 512
        masks = at("masks", [P, 7, 2 * P], I8, o); o += 7 * 256
        wgu = at("wgu", [RANK + 1, 2, GK], F32, o); o += 8192
        lrT = at("lrT", [RANK + 1, 2, T], F32, o); o += 2048
        diag2 = at("diag2", [P, 2 * P], F32, o); o += 1024
        assert o - ov <= room, (o - ov, room)
        xagain = at("xagain", [P, 2, D], F32, phase)
        o = phase
        hid_hi = at("hid_hi", [P, 24, T], F32R, o); o += 24576
        hid_lo = at("hid_lo", [P, 24, T], F32R, o); o += 24576
        assert o - ov <= room, (o - ov, room)
        pT_hi = at("pT_hi", [P, 2, T], F32R, phase + 20 * 1024)
        pT_lo = at("pT_lo", [P, 2, T], F32R, phase + 24576 + 20 * 1024)
        p_tok = at("p_tok", [P, 2, T], F32, gates_at)
        PPJ = at("PPJ", [P, 2, D], F32, phase)
        fn_bc = at("fn_bc", [P, D], F32, phase + 24576)
        o = phase
        GB = at("GB", [P, 2, D], F32, o)
        windows = at("windows", [P, 4, 384], F32, o)
        small = o + 8192
        o += 16384
        U = at("U", [P, 2, 1024], F32, o)
        ZB = at("ZB", [P, 2, 1024], F32, o + 8192)
        VA = at("VA", [P, 2, MH, VW], F32, o)
        GA = at("GA", [P, 2, D], F32, o); o += 2 * MH * VW * 4
        yb_hi = at("yb_hi", [P, 8, T], F32R, o)
        npw_bc = at("npw_bc", [P, D], F32, o); o += 8192
        yb_lo = at("yb_lo", [P, 8, T], F32R, o); o += 8192
        W = at("W", [P, 384], F32, o); o += 1536
        PT = at("PT", [P, 384], F32, o); o += 1536
        aR = at("aR", [MH, T], F32, o); o += 1024
        bT = at("bT", [P, 2, MH], F32, o); o += 64
        emT = at("emT", [P, 2, MH], F32, o); o += 64
        den = at("den", [P, 2], F32, o); o += 32
        rden = at("rden", [P, 2], F32, o); o += 32
        assert o - ov <= room, (o - ov, room)
        qk2T = at("qk2T", [P, 32, T], F32, xb_at)
        conv = at("conv", [P, 4, T], F32, gates_at)
        gate_bias = at("gate_bias", [P, 2 * MH], F32, small)
        gi = at("gi", [P, 2, 2 * MH], F32, small + 64)
        minus_abs_f = at("minus_abs_f", [P, 2, MH], F32, small + 192)
        lnf = at("lnf", [P, 2, MH], F32, small + 256)
        logf = at("logf", [P, 2, MH], F32, small + 320)
        iR = at("iR", [MH, T], F32, small + 1024)
        fR = at("fR", [MH, T], F32, small + 2048)
        ones8 = at("ones8", [MH, T], F32, small + 3072)
        Fc = at("Fc", [MH, T], F32, small + 4096)
        mR = at("mR", [MH, T], F32, small + 5120)
        bR = at("bR", [MH, T], F32, small + 6144)
        emR = at("emR", [MH, T], F32, small + 7168)
        OUT = at("OUT", [P, 2, D], F32, xb_at)

        acc = [[ctx.enter_context(nc.psum_tensor(f"acc{a}{b}", [P, NC], F32)) for b in range(2)]
               for a in range(2)]
        tp = [ctx.enter_context(nc.psum_tensor(f"tp{b}", [P, NC], F32)) for b in range(2)]
        mx = [ctx.enter_context(nc.psum_tensor(f"mx{b}", [P, NC], F32)) for b in range(2)]

        def sem(name):
            return ctx.enter_context(nc.semaphore(name))

        landed = [sem(f"landed{i}") for i in range(RAW_SLOTS)]
        hi_ready, lo_ready, consumed = sem("hi_ready"), sem("lo_ready"), sem("consumed")
        evac = [sem("evac0"), sem("evac1")]
        tp_ready = sem("tp_ready")
        tp_read = [sem("tp_read0"), sem("tp_read1")]
        xt_hi = sem("xt_hi")
        ms_ready, rstd_ready, squared = sem("ms_ready"), sem("rstd_ready"), sem("squared")
        loads = {k: sem(f"load_{k}") for k in (
            "ident", "vec", "sums", "masks", "diag", "wgu", "xagain", "p", "fn", "windows", "gbias",
            "npw", "out")}
        x_landed = [sem(f"x_landed{i}") for i in range(4)]
        act_self, dve_self = sem("act_self"), sem("dve_self")
        half_set, ones_row_set, ones_set = sem("half_set"), sem("ones_row_set"), sem("ones_set")
        masks_ready = sem("masks_ready")
        gk_ready, gk_read, gk_min, gk_exp, gk_ln, g_ready = (
            sem("gk_ready"), sem("gk_read"), sem("gk_min"), sem("gk_exp"), sem("gk_ln"), sem("g_ready"))
        og_silu = sem("og_silu")
        e_ready, ex_ready, xq_ready, xk_ready = sem("e_ready"), sem("ex_ready"), sem("xq_ready"), sem("xk_ready")
        p_ready, a_ready = sem("p_ready"), sem("a_ready")
        ho_ms, ho_rstd = sem("ho_ms"), sem("ho_rstd")
        f_gate = sem("f_gate")
        sgp_ready, h_ready = sem("sgp_ready"), sem("h_ready")
        hf_ready = [sem("hf_ready0"), sem("hf_ready1")]
        s2_ready = sem("s2_ready")
        abs_ready, ln_ready, logf_ready, scan_ready, em_ready = (
            sem("abs_ready"), sem("ln_ready"), sem("logf_ready"), sem("scan_ready"), sem("em_ready"))
        qk2_ready = sem("qk2_ready")
        oz_sg, oz_prod = sem("oz_sg"), sem("oz_prod")
        s_ready, w_ready, wexp_ready, wmask_ready, pt_ready = (
            sem("s_ready"), sem("w_ready"), sem("wexp_ready"), sem("wmask_ready"), sem("pt_ready"))
        ya_ready = [sem("ya_ready0"), sem("ya_ready1")]
        merged_ready = [sem("merged_ready0"), sem("merged_ready1")]
        x2_ready, y_ready = sem("x2_ready"), sem("y_ready")

        block = ctx.enter_context(nc.Block())

        def gran(job, n, j):
            return job.g0 + n * job.G + j

        def width(job, kc):
            return kc * job.w

        def cols(n, size=NC):
            return slice(n * size, (n + 1) * size) if isinstance(n, int) else bass.ds(n * size, size)

        def acc_of(job, ns):
            return acc[(job.t0 + ns) % 2]

        def done(job, n):
            return gran(job, n + 1, 0)

        def E(job, n):
            return job.t0 + n + 1

        def JE(job):
            return min(3, job.G - 1)

        def JT(job, prev_name):
            return min(5 if prev_name == "pg" else 3, job.G - 1)

        def JV(job, prev_name):
            return min(7 if prev_name == "pg" else 6, job.G - 1)

        def vcol(name, k):
            a = VEC[name][0] + k
            return vec[:, a:a + 1]

        NORM_OF = {"x": "mixer_norm", "wo": "ffn_norm", "f2o": "ple_norm",
                   "pg": "norm_pre", "ya": "mlstm_norm", "pool": "pool_scale", "y": "gla_out_norm"}
        DEST = {"x": (xa_hi, xa_lo), "y": (xb_hi, xb_lo), "wo": (xa_hi, xa_lo), "f2o": (xb_hi, xb_lo),
                "pg": (xa_hi, xa_lo), "ub": (xb_hi, xb_lo), "ya": (xb_hi, xb_lo), "pm": (xa_hi, xa_lo),
                "pool": (yb_hi, yb_lo), "pt": (pT_hi, pT_lo), "f1": (hid_hi, hid_lo), "f2": (hid_hi, hid_lo)}

        def xt_part(job, part, k):
            src = {"f1o": "f1", "f2o": "f2", "lr": "x", "qk": "x", "v": "x", "og": "x", "wo": "y", "f1": "wo", "f2": "wo",
                   "pp": "pt", "pg": "f2o", "ub": "pg", "zb": "pg", "pool": "ub", "if": "pg",
                   "qk2": "pg", "v2": "pg", "oz": "pg", "gb": "pg", "ga": "pg", "pb": "pool",
                   "pm": "ya", "out": "pm"}[job.name]
            return DEST[src][part][:, k, :]

        def needs(job, j):
            name = job.name
            by_bank = {"lr": "x", "wo": "y", "f1": "wo", "pg": "f2o", "ub": "pg", "out": "pm"}
            if name in by_bank:
                return [(J[by_bank[name]].r0 + j // 2, j % 2)]
            by_round = {"f1o": J["f1"].r0 + j, "f2o": J["f2"].r0 + j, "pp": J["pt"].r0,
                        "pool": J["ub"].r0 + 1, "pb": J["pool"].r0 + 3, "pm": J["ya"].r0 + 3}
            if name in by_round:
                return [(by_round[name], 0), (by_round[name], 1)]
            return []

        def half_size(u):
            return P if u < 2 else LEVELS[u // 2 - 1]

        def query_half(d):
            return 1 - d

        def key_half(d):
            return d

        def halves(ap, which, l):
            if l == P:
                return ap[:, :, which * P:(which + 1) * P]
            return ap.rearrange("p c (b two l) -> p c b two l", two=2, l=l)[:, :, :, which, :]

        def stage_free(job, n):
            if job.name == "qk2" and n == 0:
                return 2 * (J["if0"].r0 + 1)
            return 2 * (job.r0 + n)

        HOSTS = [("v", 1), ("v", 2), ("v", 3), ("og", 0)]

        def hosted(name, n):
            return HOSTS.index((name, n)) if (name, n) in HOSTS else None

        def after_head(name, n):
            if (name, n) == ("og", 1):
                return GH - 1
            h = hosted(name, n)
            return h - 1 if h else None

        def score(h, i):
            return h * (SCORES + 1) + i + 1

        def x_free(n):
            before = n // 2 - 2
            return score(before // SCORES, before % SCORES) + 1

        def a_block(jt, it):
            return jt if jt == it else 2 + jt

        def loop_passes(job):
            return (job.n - 2) // 2

        LOOPED = ("f1", "f2")

        SQ = {"x": 0, "gla": 8, "wo": 8 + 2 * GH, "f2o": 16 + 2 * GH, "pg": 24 + 2 * GH,
              "mlstm": 40 + 2 * GH, "out": 40 + 2 * GH + 2 * MH}

        @block.sync
        def _(sp):
            sp.dma_start(ident[:, :], c_ident).then_inc(loads["ident"], 16)
            for n in range(4):
                sp.dma_start(H[:, :, cols(n)], x[0, :, cols(n)].rearrange("(t p) d -> p t d", p=P)) \
                    .then_inc(x_landed[n], 16)

            def load(job, n, j, ns):
                g = gran(job, n, j)
                k0, kc = job.gr[j]
                slot = (job.g0 + ns * job.G + j) % RAW_SLOTS
                if not (isinstance(g, int) and g < RAW_SLOTS):
                    sp.wait_ge(lo_ready, g - RAW_SLOTS + 1)
                dst = raw[:, slot, 0:kc * job.w].rearrange("p (k n) -> p k n", k=kc)
                if job.name == "pool":
                    sp.dma_start(dst, pool_w[0, n, k0 * P:(k0 + 1) * P, :].rearrange("(k p) c -> p k c", p=P)) \
                        .then_inc(landed[slot], 16)
                    return
                src, first = SRC[job.name]
                if job.dmas == 2:
                    for a in range(2):
                        c = first(n) + a * SECOND_HALF[job.name]
                        sp.dma_start(dst[:, :, a * HF:(a + 1) * HF],
                                     src[:, k0:k0 + kc, bass.ds(c, HF)]).then_inc(landed[slot], 16)
                else:
                    sp.dma_start(dst, src[:, k0:k0 + kc, bass.ds(first(n), job.w)]) \
                        .then_inc(landed[slot], 16)

            for job in JOBS:
                if job.name in LOOPED:
                    for j in range(job.G):
                        load(job, 0, j, 0)
                    with sp.Fori(0, loop_passes(job)) as i:
                        for b in (1, 2):
                            for j in range(job.G):
                                load(job, 2 * i + b, j, b)
                    for j in range(job.G):
                        load(job, job.n - 1, j, job.n - 1)
                else:
                    for n in range(job.n):
                        for j in range(job.G):
                            load(job, n, j, n)
            for n in range(4):
                for t in range(2):
                    sp.wait_ge(y_ready, 2 * n + t + 1)
                    sp.dma_start(out[0, t * P:(t + 1) * P, cols(n)], OUT[:, t, cols(n)]) \
                        .then_inc(loads["out"], 16)
            sp.wait_ge(loads["out"], 16 * 8)

        @block.gpsimd
        def _(pool):
            nc.gpsimd.memset(half[:, :], -0.5).then_inc(half_set, 1)
            nc.gpsimd.memset(lrT[:, :, :], 1.0).then_inc(ones_row_set, 1)
            pool.wait_ge(half_set, 1)

            def inverse_root(i):
                pool.wait_ge(ms_ready, i + 1)
                nc.gpsimd.tensor_tensor(rstd[:, i, :], msq[:, i, :], half[:, 0:2], ALU.pow) \
                    .then_inc(rstd_ready, 1)

            pool.wait_ge(loads["masks"], 16)
            for t in range(2):
                nc.gpsimd.tensor_copy(masks[:, :, t * P:(t + 1) * P], masks_raw[:, :, :]) \
                    .then_inc(masks_ready, 1)

            def head_root(h):
                pool.wait_ge(ho_ms, h + 1)
                nc.gpsimd.tensor_tensor(hrs[:, 2 * h:2 * h + 2], hms[:, 2 * h:2 * h + 2], half[:, 0:2],
                                        ALU.pow).then_inc(ho_rstd, 1)

            inverse_root(0)
            for h in range(GH):
                for u in range(UNITS):
                    if h and u == 4:
                        head_root(h - 1)
                    l, c = half_size(u), u % 2
                    n = h * UNITS + u
                    pool.wait_ge(ex_ready, n + 1)
                    if n == 0:
                        for b in range(2):
                            pool.wait_ge(tp_read[b], J["qk"].r0 + 4)
                    if n >= 4:
                        pool.wait_ge(p_ready, x_free(n))
                    for d in range(2):
                        ins = nc.gpsimd.tensor_tensor(
                            halves(X[:, (n // 2) % 2, 1, c:c + 1, :], key_half(d), l),
                            halves(qkT[:, 8 + 2 * h + c:9 + 2 * h + c, :], key_half(d), l),
                            halves(Ex[:, d:d + 1, :], key_half(d), l), ALU.mult)
                    ins.then_inc(xk_ready, 1)
            head_root(GH - 1)
            inverse_root(1)
            inverse_root(2)
            for n in range(4):
                for t in range(2):
                    pool.wait_ge(evac[t], E(J["pg"], n))
                nc.gpsimd.tensor_tensor(gates[:, :, :], gates[:, :, :], PPJ[:, :, cols(n)], ALU.mult) \
                    .then_inc(sgp_ready, 1)
            inverse_root(3)
            inverse_root(4)
            pool.wait_ge(rstd_ready, 4)
            pool.wait_ge(tp_ready, 2 * (J["pg"].r0 + 4))
            pool.wait_ge(squared, SQ["pg"] + 16)
            for t in range(2):
                nc.gpsimd.tensor_scalar(H[:, t, :], H[:, t, :], rstd[:, 3, t:t + 1], None, ALU.mult) \
                    .then_inc(x2_ready, 1)
            for t in range(2):
                pool.wait_ge(evac[t], E(J["pool"], 3))
            nc.gpsimd.memset(VA[:, :, :, MD:VW], 1.0).then_inc(ones_set, 1)
            nc.gpsimd.memset(ones8[:, :], 1.0).then_inc(ones_set, 1)
            for h in range(MH):
                pool.wait_ge(wexp_ready, h + 1)
                for c in (0, T):
                    nc.gpsimd.affine_select(out=W[:, c:c + P], in_=W[:, c:c + P], compare_op=ALU.is_ge,
                                            fill=0.0, base=0, pattern=[[1, P]], channel_multiplier=-1) \
                        .then_inc(wmask_ready, 1)
            pool.wait_ge(ho_ms, GH + 1)
            nc.gpsimd.tensor_tensor(hrs[:, :], hms[:, :], half[:, :], ALU.pow).then_inc(ho_rstd, 1)
            inverse_root(5)

        @block.scalar
        def _(act):
            def split_hi(job, n, j, ns):
                g = gran(job, n, j)
                kc = job.gr[j][1]
                sg = job.g0 + ns * job.G + j
                slot, hl = sg % RAW_SLOTS, sg % HL_SLOTS
                visit = n if job.name in LOOPED else (n * job.G + j) // RAW_SLOTS
                act.wait_ge(landed[slot], visit * (16 * job.dmas) + job.landed0[slot] + 16 * job.dmas)
                if not (isinstance(g, int) and g < HL_SLOTS):
                    act.wait_ge(consumed, g - HL_SLOTS + 1)
                nc.scalar.copy(w_hi[:, hl, 0:kc * job.w], raw[:, slot, 0:kc * job.w]).then_inc(hi_ready, 1)

            def xt_high(name, n, k_of, scale, full):
                r = J[name].r0 + n
                hi = DEST[name][0]
                for b in range(2):
                    act.wait_ge(tp_ready, 2 * r + b + 1)
                    k = k_of(b)
                    if scale is None:
                        ins = nc.scalar.copy(hi[:, bass.ds(k, full), :],
                                             tp[b][:, 0:full * T].rearrange("p (k t) -> p k t", k=full))
                    else:
                        for f in range(full):
                            ins = nc.scalar.activation(hi[:, k + f, :], tp[b][:, f * T:(f + 1) * T],
                                                       ACT.Copy, scale=scale(k + f))
                    ins.then_inc(xt_hi, 1)

            def squares(i, dst, src):
                if i:
                    act.wait_ge(squared, i)
                nc.scalar.activation(junk[:, 0:src.shape[-1]], src, ACT.Square, accum_out=dst) \
                    .then_inc(squared, 1)

            def evacuate(job, n, ns):
                name = job.name
                a = acc_of(job, ns)
                if name in ("f1o", "pool", "if", "pb", "pm"):
                    return
                act.wait_ge(consumed, done(job, n))
                if name == "lr":
                    nc.scalar.copy(stage[0:2 * RANK, 0, 0:P], a[0][0:2 * RANK, 0:P]).then_inc(evac[0], 1)
                elif name in ("qk", "v", "qk2", "v2", "ub", "pp"):
                    w = job.w
                    scale = None if name == "pp" else rstd[:, 0 if name in ("qk", "v") else S2, 0:1]
                    dst = {"qk": stage, "qk2": stage, "v": V, "v2": VA, "ub": U, "pp": PPJ}[name]
                    src = a[0][:, 0:w]
                    if name in ("qk", "qk2"):
                        act.wait_ge(tp_ready, stage_free(job, n))
                    if name == "v":
                        act.wait_ge(g_ready, 8)
                    if name == "ub":
                        act.wait_ge(s2_ready, 1)
                        act.wait_ge(hf_ready[1], 4)
                    if name == "v2":
                        dst, src = dst[:, 0, 2 * n:2 * n + 2, 0:MD], src.rearrange("p (h d) -> p h d", h=2)
                    elif dst is stage:
                        dst = dst[:, 0, 0:w]
                    else:
                        dst = dst[:, 0, cols(n)]
                    if scale is None:
                        nc.scalar.copy(dst, src).then_inc(evac[0], 1)
                    else:
                        nc.scalar.activation(dst, src, ACT.Copy, scale=scale).then_inc(evac[0], 1)
                elif name == "zb":
                    for t in range(2):
                        nc.scalar.activation(ZB[:, t, cols(n)], a[t][:, :], ACT.Silu,
                                             scale=rstd[:, S2, t:t + 1]).then_inc(evac[t], 1)
                elif name == "og":
                    for t in range(2):
                        act.wait_ge(evac[t], E(job, n) - 1)
                        nc.scalar.activation(gates[:, t, :], a[t][:, :], ACT.Silu,
                                             scale=rstd[:, 0, t:t + 1]).then_inc(og_silu, 1)
                elif name in ("f1", "f2"):
                    act.wait_ge(rstd_ready, 2)
                    for t in range(2):
                        act.wait_ge(evac[t], E(job, n) - 1)
                        nc.scalar.activation(gates[:, t, 0:HF], a[t][:, 0:HF], ACT.Silu,
                                             scale=rstd[:, 1, t:t + 1]).then_inc(f_gate, 1)
                elif name in ("wo", "f2o"):
                    for t in range(2):
                        act.wait_ge(evac[t], E(job, n))
                        squares(SQ[name] + 2 * n + t, ssq[:, 1 if name == "wo" else 2, t, n:n + 1],
                                H[:, t, cols(n)])
                elif name == "pg":
                    act.wait_ge(rstd_ready, 3)
                    for t in range(2):
                        if n:
                            act.wait_ge(h_ready, 2 * n)
                        nc.scalar.activation(gates[:, t, :], a[t][:, :], ACT.Sigmoid,
                                             scale=rstd[:, 2, t:t + 1]).then_inc(evac[t], 1)
                elif name == "oz":
                    if n == 0:
                        act.wait_ge(qk2_ready, 16)
                    for t in range(2):
                        act.wait_ge(evac[t], E(job, n) - 1)
                        nc.scalar.activation(gates[:, t, :], a[t][:, :], ACT.Sigmoid,
                                             scale=rstd[:, S2, t:t + 1]).then_inc(oz_sg, 1)
                elif name in ("gb", "ga"):
                    dst = GB if name == "gb" else GA
                    for t in range(2):
                        act.wait_ge(ya_ready[t], n + 1 if name == "gb" else 4)
                        nc.scalar.activation(dst[:, t, cols(n)], a[t][:, :], ACT.Sigmoid,
                                             scale=rstd[:, S2, t:t + 1]).then_inc(evac[t], 1)
                elif name == "out":
                    for t in range(2):
                        squares(SQ["out"] + 2 * n + t, ssq[:, 5, t, n:n + 1], a[t][:, :])

            def evacuate_transposed(job, n):
                name = job.name
                if name == "qk":
                    act.wait_ge(tp_ready, 2 * (job.r0 + n) + 1)
                    nc.scalar.activation(qkT[:, 4 * n:4 * n + 2, :],
                                         tp[0][:, :].rearrange("p (k t) -> p k t", k=2), ACT.Copy,
                                         scale=GDK ** -0.5 if n < 2 else 1.0).then_inc(tp_read[0], 1)
                elif name == "og":
                    xt_high("y", n, lambda b: 4 * n + 2 * b, lambda k: vcol("gla_out_norm", k % 4), 2)
                elif name in ("wo", "f2o", "pg"):
                    xt_high(name, n, lambda b: 4 * n + 2 * b, lambda k: vcol(NORM_OF[name], k), 2)
                elif name in ("ub", "pm"):
                    xt_high(name, n, lambda b: 4 * n + 2 * b, None, 2)
                elif name in ("f1", "f2"):
                    xt_high(name, n, lambda b: 2 * n + b, None, 1)
                elif name == "pool":
                    xt_high(name, n, lambda b: 2 * n + b, lambda k: vcol("pool_scale", k), 1)

            def qk2_silu(n):
                for b in range(2):
                    act.wait_ge(tp_read[b], J["qk2"].r0 + n + 1)
                    nc.scalar.activation(qk2T[:, 4 * n + 2 * b:4 * n + 2 * b + 2, :],
                                         conv[:, 2 * b:2 * b + 2, :], ACT.Silu).then_inc(qk2_ready, 1)

            def gk_exp_of(i):
                t, z, c = i // 4, (i // 2) % 2, i % 2
                act.wait_ge(gk_read, i + 1)
                nc.scalar.activation(G[:, t, z, cols(c)], G[:, t, z, cols(c)], ACT.Exp) \
                    .then_inc(gk_exp, 1)

            def gk_ln_of(i):
                t, z, c = i // 4, (i // 2) % 2, i % 2
                act.wait_ge(gk_exp, i + 1)
                nc.scalar.activation(G[:, t, z, cols(c)], G[:, t, z, cols(c)], ACT.Ln, bias=1.0) \
                    .then_inc(gk_ln, 1)

            def gla_exp(h, u):
                n = h * UNITS + u
                act.wait_ge(e_ready, n + 1)
                if n:
                    act.wait_ge(xq_ready, n)
                    act.wait_ge(xk_ready, n)
                nc.scalar.activation(Ex[:, :, :], mx[0][:, :].rearrange("p (d t) -> p d t", d=2), ACT.Exp,
                                     scale=1.0 / GATE_NORM).then_inc(ex_ready, 1)

            def gla_squares(h):
                for t in range(2):
                    act.wait_ge(tp_ready, 2 * (J["o"].r0 + h) + t + 1)
                    squares(SQ["gla"] + 2 * h + t, hss[:, 2 * h + t:2 * h + t + 1], tp[t][:, :])

            def mlstm_squares(h):
                for t in range(2):
                    act.wait_ge(tp_read[t], J["num"].r0 + h + 1)
                    squares(SQ["mlstm"] + 2 * h + t, hss[:, 2 * h + t:2 * h + t + 1], VA[:, t, h, 0:MD])

            def after_split(job, n, j, ns):
                name = job.name
                pj, pn, pns = (job.prev, job.prev.n - 1 if job.prev else 0, job.prev.n - 1 if job.prev else 0) \
                    if ns == 0 else (job, n - 1, ns - 1)
                if name == "qk" and n == 2:
                    gk_exp_of(j)
                if name == "qk" and n == 3:
                    gk_ln_of(j)
                if hosted(name, n) is not None and j >= LAG:
                    for u in (2 * (j - LAG), 2 * (j - LAG) + 1):
                        gla_exp(hosted(name, n), u)
                if after_head(name, n) is not None:
                    h = after_head(name, n)
                    if j < LAG:
                        for u in (2 * (j - LAG + 8), 2 * (j - LAG + 8) + 1):
                            gla_exp(h, u)
                    if j == LAG + 1:
                        gla_squares(h)
                if name == "qk2" and n >= 2 and j == 0:
                    qk2_silu(n - 2)
                if name == "v2" and n < 2 and j == 0:
                    qk2_silu(6 + n)
                if name == "oz" and n >= 1 and j == 1:
                    mlstm_squares(n - 1)
                if name == "gb" and n == 0 and j == 1:
                    mlstm_squares(MH - 1)
                if name == "oz" and j == 4:
                    act.wait_ge(w_ready, n + 1)
                    nc.scalar.activation(W[:, :], W[:, :], ACT.Exp).then_inc(wexp_ready, 1)
                if pj is not None and j == JE(job):
                    evacuate(pj, pn, pns)
                if pj is not None and pj.name == "pg" and j == 5:
                    for t in range(2):
                        act.wait_ge(h_ready, 2 * pn + t + 1)
                        squares(SQ["pg"] + 4 * pn + t, ssq[:, 3, t, pn:pn + 1], H[:, t, cols(pn)])
                if pj is not None and pj.name == "pg" and j == 6:
                    for t in range(2):
                        act.wait_ge(hf_ready[t], pn + 1)
                        squares(SQ["pg"] + 4 * pn + 2 + t, ssq[:, 4, t, pn:pn + 1], H[:, t, cols(pn)])
                if name == "f2o" and n == 1 and j == JV(job, "") - 1:
                    xt_high("pt", 0, lambda b: b, None, 1)
                if pj is not None and j == JV(job, pj.name):
                    evacuate_transposed(pj, pn)
                if name == "qk" and n == 0 and j == 5:
                    act.wait_ge(rstd_ready, 1)
                    act.wait_ge(tp_ready, 2 * J["lr0"].r0 + 1)
                    nc.scalar.activation(stage[:, 0, P:P + 2 * RANK], tp[0][:, 0:2 * RANK], ACT.Copy,
                                         scale=rstd[:, 0, 0:1]).then_inc(tp_read[0], 1)
                if name == "gb" and j == 7:
                    xt_high("ya", n, lambda b: 4 * n + 2 * b, lambda k: vcol("mlstm_norm", k), 2)
                if name == "qk" and n == 0 and j == 7:
                    act.wait_ge(tp_ready, 2 * J["lr"].r0 + 1)
                    act.wait_ge(ones_row_set, 1)
                    nc.scalar.copy(lrT[0:RANK, 0, :], tp[0][0:RANK, 0:T]).then_inc(tp_read[0], 1)
                if name == "qk2" and n == 0 and j == 6:
                    act.wait_ge(abs_ready, 1)
                    nc.scalar.activation(lnf[:, :, :], minus_abs_f[:, :, :], ACT.Exp).then_inc(act_self, 1)
                    act.wait_ge(act_self, 1)
                    nc.scalar.activation(lnf[:, :, :], lnf[:, :, :], ACT.Ln, bias=1.0).then_inc(ln_ready, 1)
                if name == "qk2" and n == 1 and j == 3:
                    act.wait_ge(scan_ready, 1)
                    nc.scalar.activation(emR[:, :], mR[:, :], ACT.Exp, scale=-1.0).then_inc(em_ready, 1)
                if name == "og" and n == 1 and j == LAG + 2:
                    act.wait_ge(p_ready, GH * (SCORES + 1))
                    act.wait_ge(xq_ready, GH * UNITS)
                    act.wait_ge(xk_ready, GH * UNITS)
                    act.dma_start(xagain[:, :, :], x[0].rearrange("(t p) d -> p t d", p=P)) \
                        .then_inc(loads["xagain"], 16)
                if name == "f2o" and n == 0 and j == job.G - 1:
                    for t in range(2):
                        act.wait_ge(evac[t], E(J["f2"], 9))
                    act.dma_start(p_tok[:, :, :], p[0, 0].rearrange("(t p) d -> p t d", p=P)) \
                        .then_inc(loads["p"], 16)
                if name == "pp" and n == 1:
                    act.wait_ge(consumed, done(J["f2o"], 3))
                    act.dma_start(fn_bc[:, :], final_norm.rearrange("(a d) -> a d", a=1)
                                  .broadcast_to([P, D])).then_inc(loads["fn"], 16)
                if name == "ub" and n == 0 and j == 7:
                    act.wait_ge(sgp_ready, 4)
                    act.dma_start(windows[:, :, :], c_windows.rearrange("p (g t) -> p g t", g=4)) \
                        .then_inc(loads["windows"], 16)
                    act.dma_start(gate_bias[:, 0:MH], i_bias.broadcast_to([P, MH])) \
                        .then_inc(loads["gbias"], 16)
                    act.dma_start(gate_bias[:, MH:2 * MH], f_bias.broadcast_to([P, MH])) \
                        .then_inc(loads["gbias"], 16)
                if name == "pm" and n == 0 and j == 0:
                    act.wait_ge(consumed, done(J["pb"], 3))
                    act.dma_start(npw_bc[:, :], norm_post.broadcast_to([P, D])).then_inc(loads["npw"], 16)

            act.dma_start(vec_raw[:, 0, :], conv_w[0].rearrange("w (f p) -> (w f) p", p=P)) \
                .then_inc(loads["vec"], 16)
            at_row = 0
            for ap in (mixer_norm, gla_out_norm, ffn_norm, ple_norm, final_norm, norm_pre, pool_scale,
                       mlstm_norm):
                flat = ap if len(ap.shape) == 1 else ap[0]
                n = flat.shape[0] // P
                act.dma_start(vec_raw[at_row:at_row + n, 1, :], flat.rearrange("(f p) -> f p", p=P)) \
                    .then_inc(loads["vec"], 16)
                at_row += n
            act.dma_start(vec_raw[0:32, 2, :], conv_b[0].rearrange("(f p) -> f p", p=P)) \
                .then_inc(loads["vec"], 16)
            act.dma_start(wgu[0:RANK, :, :], gla_w_gate_up[0].rearrange("z r d -> r z d")) \
                .then_inc(loads["wgu"], 16)
            act.dma_start(wgu[RANK:RANK + 1, :, :], gla_b_gate).then_inc(loads["wgu"], 16)
            act.dma_start(sums[:, :, :], c_sums.rearrange("p (a b) -> p a b", b=P)).then_inc(loads["sums"], 16)
            act.dma_start(masks_raw[:, :, :], c_masks.rearrange("p (a i) -> p a i", a=7)) \
                .then_inc(loads["masks"], 16)
            act.dma_start(diag2[:, :], c_diag).then_inc(loads["diag"], 16)
            for j in range(HL_SLOTS):
                split_hi(J["lr"], 0, j, 0)
            act.wait_ge(tp_read[1], 1)
            for r in range(4):
                xt_high("x", r, lambda b: 4 * r + 2 * b, lambda k: vcol("mixer_norm", k), 2)
            for n in range(4):
                act.wait_ge(x_landed[n], 16)
                for t in range(2):
                    squares(SQ["x"] + 2 * n + t, ssq[:, 0, t, n:n + 1], H[:, t, cols(n)])

            for job in JOBS:
                def column_tile(n, ns):
                    for j in range(job.G):
                        if not (job.name == "lr" and j < HL_SLOTS):
                            split_hi(job, n, j, ns)
                        after_split(job, n, j, ns)
                if job.name in LOOPED:
                    column_tile(0, 0)
                    with act.Fori(0, loop_passes(job)) as i:
                        for b in (1, 2):
                            column_tile(2 * i + b, b)
                    column_tile(job.n - 1, job.n - 1)
                else:
                    for n in range(job.n):
                        column_tile(n, n)
            evacuate(J["out"], 3, 3)

        @block.tensor
        def _(pe):
            def product(job, n, j, ns):
                g = gran(job, n, j)
                k0, kc = job.gr[j]
                hl = (job.g0 + ns * job.G + j) % HL_SLOTS
                w = job.w
                a = acc_of(job, ns)
                if j == 0 and not (isinstance(n, int) and job.t0 + n < 2):
                    for t in range(2):
                        pe.wait_ge(evac[t], E(job, n) - 2)
                if ns == 0:
                    for r, b in needs(job, j):
                        pe.wait_ge(tp_read[b], r + 1)
                pe.wait_ge(lo_ready, g + 1)
                for kk in range(kc):
                    k = k0 + kk
                    kx = 2 * n + k if job.name == "pool" else k
                    hi = w_hi[:, hl, kk * w:(kk + 1) * w]
                    lo = w_lo[:, hl, kk * w:(kk + 1) * w]
                    first = j == 0 and kk == 0
                    last = j == job.G - 1 and kk == kc - 1
                    if job.name in ("lr", "if"):
                        xh, xl = xt_part(job, 0, kx), xt_part(job, 1, kx)
                        nc.tensor.matmul(a[0][0:w, 0:T], hi, xh, start=first, stop=False)
                        nc.tensor.matmul(a[0][0:w, 0:T], lo, xh, start=False, stop=False)
                        ins = nc.tensor.matmul(a[0][0:w, 0:T], hi, xl, start=False, stop=last)
                        if kk == kc - 1:
                            ins.then_inc(consumed, 1)
                        continue
                    for t in range(2):
                        xh = xt_part(job, 0, kx)[:, t * P:(t + 1) * P]
                        xl = xt_part(job, 1, kx)[:, t * P:(t + 1) * P]
                        nc.tensor.matmul(a[t][:, 0:w], xh, hi, start=first, stop=False)
                        nc.tensor.matmul(a[t][:, 0:w], xh, lo, start=False, stop=False)
                        ins = nc.tensor.matmul(a[t][:, 0:w], xl, hi, start=False, stop=last)
                    if kk == kc - 1:
                        ins.then_inc(consumed, 1)
                    if hosted(job.name, n) is not None:
                        gla_step(hosted(job.name, n), k)
                    if (job.name, n) == ("og", 1):
                        if k == 0:
                            gla_scores(GH - 1, SCORES - 1)
                        if k == 3:
                            gla_output(GH - 1)

            def bank(r, b):
                if not isinstance(r, int) or r > 0:
                    pe.wait_ge(tp_read[b], r)

            def transpose_round(r, src_of, per_bank=2):
                for b in range(2):
                    bank(r, b)
                    for f in range(per_bank):
                        for t in range(2):
                            ins = nc.tensor.transpose(tp[b][:, f * T + t * P:f * T + (t + 1) * P],
                                                      src_of(b * per_bank + f, t), ident[:, :])
                    ins.then_inc(tp_ready, 1)

            def transposes(job, n):
                name = job.name
                if name not in ("lr", "qk", "og", "qk2", "pm", "wo", "f2o", "pg", "f1", "f2", "pool", "ub", "if"):
                    return
                for t in range(2):
                    if name == "pg":
                        pe.wait_ge(hf_ready[t], n + 1)
                    elif name == "pm":
                        pe.wait_ge(merged_ready[t], n + 1)
                    else:
                        pe.wait_ge(evac[t], E(job, n))
                r = J["y"].r0 + n if name == "og" else job.r0 + n
                if name in ("lr", "if"):
                    r, w = J[name + "0"].r0, job.w
                    for t in range(2):
                        bank(r, t)
                        nc.tensor.transpose(tp[t][:, 0:w], stage[0:w, t, 0:P], ident[0:w, 0:w]) \
                            .then_inc(tp_ready, 1)
                elif name in ("qk", "qk2", "pm"):
                    transpose_round(r, lambda f, t: stage[:, t, f * P:(f + 1) * P])
                elif name in ("og", "wo", "f2o", "pg"):
                    transpose_round(r, lambda f, t: H[:, t, n * NC + f * P:n * NC + (f + 1) * P])
                elif name in ("f1", "f2", "pool"):
                    transpose_round(r, lambda f, t: stage[:, t, f * P:(f + 1) * P], 1)
                elif name == "ub":
                    pe.wait_ge(loads["windows"], 16)
                    for b in range(2):
                        bank(r, b)
                        for f in range(2):
                            c = 4 * n + 2 * b + f
                            w = windows[:, c // 2, :]
                            nc.tensor.matmul(tp[b][:, f * T:(f + 1) * T], U[:, 0, c * P:(c + 1) * P],
                                             w[:, 0:T], start=True, stop=False, skip_group_check=True)
                            ins = nc.tensor.matmul(tp[b][:, f * T + P:(f + 1) * T], U[:, 1, c * P:(c + 1) * P],
                                                   w[:, T:T + P], start=False, stop=True, skip_group_check=True)
                        ins.then_inc(tp_ready, 1)

            def lr_back():
                r = J["lr"].r0
                for z in range(2):
                    for t in range(2):
                        bank(r, t)
                    for t in range(2):
                        ins = nc.tensor.transpose(tp[z][0:RANK, t * P:(t + 1) * P],
                                                  stage[:, t, P + z * RANK:P + (z + 1) * RANK], ident[:, :])
                    ins.then_inc(tp_ready, 1)

            def gk_piece(i):
                t, z, c = i // 4, (i // 2) % 2, i % 2
                if i == 0:
                    for b in range(2):
                        pe.wait_ge(tp_read[b], J["lr"].r0 + 1)
                    pe.wait_ge(loads["wgu"], 32)
                if i >= 2:
                    pe.wait_ge(gk_read, i - 1)
                nc.tensor.matmul(mx[i % 2][:, :], lrT[:, z, t * P:(t + 1) * P], wgu[:, z, cols(c)],
                                 start=True, stop=True).then_inc(gk_ready, 1)

            def gla_sums(h, u):
                c = u % 2
                n = h * UNITS + u
                if n == 0:
                    pe.wait_ge(loads["sums"], 16)
                    pe.wait_ge(gk_read, 8)
                    pe.wait_ge(g_ready, 8)
                else:
                    pe.wait_ge(ex_ready, n)
                for d in range(2):
                    for t in range(2):
                        m = sums[:, 9 * d + (t if u < 2 else u // 2 + 1), :]
                        ins = nc.tensor.matmul(mx[0][:, d * T + t * P:d * T + (t + 1) * P],
                                               G[:, t, d, h * GDK + c * P:h * GDK + (c + 1) * P], m,
                                               start=True, stop=True)
                ins.then_inc(e_ready, 1)

            def score_bank(m):
                if m:
                    pe.wait_ge(a_ready, m)
                return mx[1]

            def gla_diagonal(h):
                if h == 0:
                    for b in range(2):
                        pe.wait_ge(tp_read[b], J["qk"].r0 + 4)
                to = score_bank(score(h, -1))
                for t in range(2):
                    s = slice(t * P, (t + 1) * P)
                    for c in range(2):
                        ins = nc.tensor.matmul(to[:, t * P:(t + 1) * P], qkT[:, 8 + 2 * h + c, s],
                                               qkT[:, 2 * h + c, s], start=(c == 0), stop=(c == 1))
                ins.then_inc(p_ready, 1)

            def gla_scores(h, i):
                n = h * UNITS + 2 * i
                pe.wait_ge(xq_ready, n + 2)
                pe.wait_ge(xk_ready, n + 2)
                to = score_bank(score(h, i))
                xq, xk = X[:, (n // 2) % 2, 0, :, :], X[:, (n // 2) % 2, 1, :, :]
                for t in range(2):
                    it = 1 - t if i == 0 else t
                    for c in range(2):
                        ins = nc.tensor.matmul(to[:, t * P:(t + 1) * P], xk[:, c, t * P:(t + 1) * P],
                                               xq[:, c, it * P:(it + 1) * P], start=(c == 0), stop=(c == 1))
                ins.then_inc(p_ready, 1)

            def gla_output(h):
                pe.wait_ge(a_ready, (h + 1) * (SCORES + 1))
                for t in range(2):
                    pe.wait_ge(evac[t], E(J["v"], h))
                for it in range(2):
                    bank(J["o"].r0 + h, it)
                    for jt in range(2):
                        ins = nc.tensor.matmul(tp[it][:, :], A_T[:, h % 2, a_block(jt, it), :], V[:, jt, cols(h, GDV)],
                                               start=(jt == 0), stop=(jt == 1))
                    ins.then_inc(tp_ready, 1)

            def gla_step(h, k):
                gla_sums(h, k)
                if k == 0 and h:
                    gla_scores(h - 1, SCORES - 1)
                if k == 1:
                    gla_diagonal(h)
                if k >= 2 and k % 2 == 0:
                    gla_scores(h, k // 2 - 1)
                if k == 3 and h:
                    gla_output(h - 1)

            def mlstm_scores(h):
                if h == 0:
                    pe.wait_ge(qk2_ready, 16)
                    pe.wait_ge(scan_ready, 1)
                else:
                    pe.wait_ge(pt_ready, h)
                nc.tensor.matmul(mx[1][:, 0:T], ident[0:MH, h:h + 1].broadcast_to([MH, P]), aR[:, :],
                                 start=True, stop=True)
                for st in range(2):
                    to = mx[0][:, 0:T] if st == 0 else mx[0][:, T:T + P]
                    for c in range(2):
                        ins = nc.tensor.matmul(to, qk2T[:, 16 + 2 * h + c, st * P:(st + 1) * P],
                                               qk2T[:, 2 * h + c, st * P:T], start=(c == 0), stop=(c == 1))
                ins.then_inc(s_ready, 1)

            def mlstm_output(h):
                r = J["num"].r0 + h
                pe.wait_ge(pt_ready, h + 1)
                if h == 0:
                    pe.wait_ge(ones_set, 2)
                for t in range(2):
                    pe.wait_ge(evac[t], E(J["v2"], h // 2))
                bank(r, 0)
                nc.tensor.matmul(tp[0][:, 0:MD + 1], PT[:, 0:P], VA[:, 0, h, 0:MD + 1],
                                 start=True, stop=True).then_inc(tp_ready, 1)
                bank(r, 1)
                nc.tensor.matmul(tp[1][:, 0:MD + 1], PT[:, P:T], VA[:, 0, h, 0:MD + 1], start=True, stop=False)
                nc.tensor.matmul(tp[1][:, 0:MD + 1], PT[:, T:T + P], VA[:, 1, h, 0:MD + 1],
                                 start=False, stop=True).then_inc(tp_ready, 1)

            def mlstm_gates():
                r = J["if"].r0
                pe.wait_ge(logf_ready, 1)
                for b, src in ((0, gi[:, :, 0:MH]), (1, logf[:, :, :])):
                    bank(r, b)
                    for t in range(2):
                        ins = nc.tensor.transpose(tp[b][0:MH, t * P:(t + 1) * P], src[:, t, :], ident[:, :])
                    ins.then_inc(tp_ready, 1)

            def mlstm_columns():
                r = J["if"].r0 + 1
                pe.wait_ge(em_ready, 1)
                for b, src in ((0, bR), (1, emR)):
                    bank(r, b)
                    for t in range(2):
                        ins = nc.tensor.transpose(tp[b][:, t * MH:(t + 1) * MH], src[:, t * P:(t + 1) * P],
                                                  ident[0:MH, 0:MH])
                    ins.then_inc(tp_ready, 1)

            def after_granule(job, n, j, ns):
                name = job.name
                pj, pn = (job.prev, job.prev.n - 1 if job.prev else 0) if ns == 0 else (job, n - 1)
                if name == "qk" and n == 1:
                    gk_piece(j)
                if name == "oz" and j == 0:
                    mlstm_scores(n)
                if name == "oz" and j == 5:
                    mlstm_output(n)
                if name == "gb" and j == 4:
                    for t in range(2):
                        pe.wait_ge(ya_ready[t], n + 1)
                    transpose_round(J["ya"].r0 + n, lambda f, t: stage[:, t, f * P:(f + 1) * P])
                if name == "f2o" and n == 1 and j == 2:
                    pe.wait_ge(loads["p"], 16)
                    transpose_round(J["pt"].r0, lambda f, t: p_tok[:, t, f * P:(f + 1) * P], 1)
                if name == "qk" and n == 0 and j == 6:
                    lr_back()
                if name == "qk2" and n == 0 and j == 7:
                    mlstm_gates()
                if name == "qk2" and n == 1 and j == 2:
                    mlstm_columns()
                if pj is not None and j == JT(job, pj.name):
                    transposes(pj, pn)

            pe.wait_ge(loads["ident"], 16)
            pe.wait_ge(loads["vec"], 160)
            nc.tensor.transpose(tp[0][:, 0:P], vec_raw[:, 0, :], ident[:, :])
            nc.tensor.transpose(tp[0][:, P:P + 32], vec_raw[0:32, 2, :], ident[0:32, 0:32]).then_inc(tp_ready, 1)
            nc.tensor.transpose(tp[1][:, 0:VEC_ROWS], vec_raw[0:VEC_ROWS, 1, :],
                                ident[0:VEC_ROWS, 0:VEC_ROWS]).then_inc(tp_ready, 1)
            for r in range(4):
                pe.wait_ge(x_landed[r], 16)
                transpose_round(J["x"].r0 + r, lambda f, t: H[:, t, r * NC + f * P:r * NC + (f + 1) * P])

            for job in JOBS:
                def column_tile(n, ns):
                    for j in range(job.G):
                        product(job, n, j, ns)
                        after_granule(job, n, j, ns)
                if job.name in LOOPED:
                    column_tile(0, 0)
                    with pe.Fori(0, loop_passes(job)) as i:
                        for b in (1, 2):
                            column_tile(2 * i + b, b)
                    column_tile(job.n - 1, job.n - 1)
                else:
                    for n in range(job.n):
                        column_tile(n, n)

        @block.vector
        def _(dve):
            own_steps = [0]

            def settle(ins):
                own_steps[0] += 1
                ins.then_inc(dve_self, 1)
                dve.wait_ge(dve_self, own_steps[0])

            def split_lo(job, n, j, ns):
                g = gran(job, n, j)
                kc = job.gr[j][1]
                sg = job.g0 + ns * job.G + j
                slot, hl = sg % RAW_SLOTS, sg % HL_SLOTS
                dve.wait_ge(hi_ready, g + 1)
                nc.vector.tensor_tensor(w_lo[:, hl, 0:kc * job.w], raw[:, slot, 0:kc * job.w],
                                        w_hi[:, hl, 0:kc * job.w].bitcast(F32), ALU.subtract) \
                    .then_inc(lo_ready, 1)

            def xt_low(name, n, k_of, scale, full):
                hi, lo = DEST[name]
                for b in range(2):
                    dve.wait_ge(xt_hi, J[name].x0 + 2 * n + b + 1)
                    k = k_of(b)
                    if scale is None:
                        ins = nc.vector.tensor_tensor(
                            lo[:, bass.ds(k, full), :],
                            tp[b][:, 0:full * T].rearrange("p (k t) -> p k t", k=full),
                            hi[:, bass.ds(k, full), :].bitcast(F32), ALU.subtract)
                    else:
                        for f in range(full):
                            ins = nc.vector.scalar_tensor_tensor(
                                out=lo[:, k + f, :], in0=tp[b][:, f * T:(f + 1) * T], scalar=scale(k + f),
                                in1=hi[:, k + f, :].bitcast(F32), op0=ALU.mult, op1=ALU.subtract)
                    ins.then_inc(tp_read[b], 1)

            def mean_square(i, count):
                dve.wait_ge(squared, count)
                settle(nc.vector.tensor_reduce(msq[:, i, :], ssq[:, i, :, :], AX.X, ALU.add))
                nc.vector.tensor_scalar(msq[:, i, :], msq[:, i, :], 1.0 / D, EPS, ALU.mult, ALU.add) \
                    .then_inc(ms_ready, 1)

            def evacuate(job, n, ns):
                name = job.name
                a = acc_of(job, ns)
                if name in ("zb", "gb", "ga"):
                    return
                dve.wait_ge(consumed, done(job, n))
                if name == "lr":
                    dve.wait_ge(evac[0], E(job, 0))
                    nc.vector.tensor_copy(stage[0:2 * RANK, 1, 0:P], a[0][0:2 * RANK, P:T]).then_inc(evac[1], 1)
                elif name in ("qk", "v", "qk2", "v2", "ub", "pp"):
                    w = job.w
                    scale = None if name == "pp" else rstd[:, 0 if name in ("qk", "v") else S2, 1:2]
                    dst = {"qk": stage, "qk2": stage, "v": V, "v2": VA, "ub": U, "pp": PPJ}[name]
                    src = a[1][:, 0:w]
                    if name in ("qk", "qk2"):
                        dve.wait_ge(tp_ready, stage_free(job, n))
                    if name == "v":
                        dve.wait_ge(g_ready, 8)
                    if name == "ub":
                        dve.wait_ge(s2_ready, 1)
                    if name == "v2":
                        dst, src = dst[:, 1, 2 * n:2 * n + 2, 0:MD], src.rearrange("p (h d) -> p h d", h=2)
                    elif dst is stage:
                        dst = dst[:, 1, 0:w]
                    else:
                        dst = dst[:, 1, cols(n)]
                    if scale is None:
                        nc.vector.tensor_copy(dst, src).then_inc(evac[1], 1)
                    else:
                        nc.vector.tensor_scalar(dst, src, scale, None, ALU.mult).then_inc(evac[1], 1)
                elif name in ("wo", "f1o", "f2o"):
                    if name == "wo":
                        dve.wait_ge(loads["xagain"], 16)
                    old = xagain if name == "wo" else H
                    for t in range(2):
                        nc.vector.tensor_tensor(H[:, t, cols(n)], a[t][:, :], old[:, t, cols(n)], ALU.add) \
                            .then_inc(evac[t], 1)
                elif name in ("f1", "f2"):
                    dve.wait_ge(tp_ready, 2 * (job.r0 + n))
                    for t in range(2):
                        dve.wait_ge(f_gate, 2 * n + (0 if name == "f1" else 2 * J["f1"].n) + t + 1)
                        nc.vector.scalar_tensor_tensor(
                            out=stage[:, t, 0:HF], in0=a[t][:, HF:2 * HF], scalar=rstd[:, 1, t:t + 1],
                            in1=gates[:, t, 0:HF], op0=ALU.mult, op1=ALU.mult).then_inc(evac[t], 1)
                elif name == "pool":
                    for t in range(2):
                        dve.wait_ge(evac[t], E(J["zb"], 1))
                    dve.wait_ge(tp_ready, 2 * (job.r0 + n))
                    for t in range(2):
                        nc.vector.tensor_tensor(stage[:, t, 0:256], a[t][:, 0:256], ZB[:, t, cols(n, 256)],
                                                ALU.mult).then_inc(evac[t], 1)
                elif name == "if":
                    dve.wait_ge(tp_ready, 2 * J["if0"].r0)
                    for t in range(2):
                        nc.vector.tensor_copy(stage[0:2 * MH, t, 0:P], a[0][0:2 * MH, t * P:(t + 1) * P]) \
                            .then_inc(evac[t], 1)
                elif name == "og":
                    for t in range(2):
                        dve.wait_ge(og_silu, 2 * n + t + 1)
                        dve.wait_ge(tp_read[t], J["o"].r0 + n + 1)
                        nc.vector.tensor_tensor(H[:, t, cols(n)], H[:, t, cols(n)], gates[:, t, :], ALU.mult) \
                            .then_inc(evac[t], 1)
                elif name == "oz":
                    for t in range(2):
                        dve.wait_ge(oz_sg, 2 * n + t + 1)
                        nc.vector.tensor_tensor(gates[:, t, 0:MD], gates[:, t, 0:MD], gates[:, t, MD:2 * MD],
                                                ALU.mult).then_inc(oz_prod, 1)
                    for t in range(2):
                        dve.wait_ge(oz_prod, 2 * n + t + 1)
                        nc.vector.scalar_tensor_tensor(
                            out=GB[:, t, cols(n, MD)], in0=a[t][:, MD:2 * MD], scalar=rstd[:, S2, t:t + 1],
                            in1=gates[:, t, 0:MD], op0=ALU.mult, op1=ALU.mult).then_inc(evac[t], 1)
                elif name == "pb":
                    for t in range(2):
                        dve.wait_ge(evac[t], E(J["gb"], n))
                        nc.vector.tensor_tensor(GB[:, t, cols(n)], a[t][:, :], GB[:, t, cols(n)], ALU.mult) \
                            .then_inc(evac[t], 1)
                elif name == "pm":
                    for t in range(2):
                        nc.vector.tensor_tensor(GA[:, t, cols(n)], a[t][:, :], GA[:, t, cols(n)], ALU.mult) \
                            .then_inc(evac[t], 1)
                    dve.wait_ge(tp_ready, 2 * (job.r0 + n))
                    for t in range(2):
                        dve.wait_ge(evac[t], E(job, n))
                        nc.vector.tensor_tensor(stage[:, t, :], GA[:, t, cols(n)], GB[:, t, cols(n)], ALU.add) \
                            .then_inc(merged_ready[t], 1)
                elif name == "out":
                    dve.wait_ge(loads["npw"], 16)
                    for t in range(2):
                        dve.wait_ge(squared, SQ["out"] + 2 * n + t + 1)
                        nc.vector.tensor_tensor(OUT[:, t, cols(n)], a[t][:, :], npw_bc[:, cols(n)], ALU.mult) \
                            .then_inc(evac[t], 1)

            def evacuate_transposed(job, n):
                name = job.name
                if name == "qk":
                    dve.wait_ge(tp_ready, 2 * (job.r0 + n) + 2)
                    nc.vector.tensor_scalar(qkT[:, 4 * n + 2:4 * n + 4, :],
                                            tp[1][:, :].rearrange("p (k t) -> p k t", k=2),
                                            GDK ** -0.5 if n < 2 else 1.0, None, ALU.mult) \
                        .then_inc(tp_read[1], 1)
                elif name == "og":
                    xt_low("y", n, lambda b: 4 * n + 2 * b, lambda k: vcol("gla_out_norm", k % 4), 2)
                elif name in ("wo", "f2o", "pg"):
                    xt_low(name, n, lambda b: 4 * n + 2 * b, lambda k: vcol(NORM_OF[name], k), 2)
                elif name in ("ub", "pm"):
                    xt_low(name, n, lambda b: 4 * n + 2 * b, None, 2)
                elif name in ("f1", "f2"):
                    xt_low(name, n, lambda b: 2 * n + b, None, 1)
                elif name == "pool":
                    xt_low(name, n, lambda b: 2 * n + b, lambda k: vcol("pool_scale", k), 1)

            def lr_transposed():
                dve.wait_ge(tp_ready, 2 * J["lr"].r0 + 2)
                dve.wait_ge(ones_row_set, 1)
                nc.vector.tensor_copy(lrT[0:RANK, 1, :], tp[1][0:RANK, 0:T]).then_inc(tp_read[1], 1)

            def convolve(n, b):
                job = J["qk2"]
                dve.wait_ge(tp_ready, 2 * (job.r0 + n) + b + 1)
                if n:
                    dve.wait_ge(qk2_ready, 2 * n)
                for tap in range(3, -1, -1):
                    s = 3 - tap
                    for f in range(2):
                        k = 4 * n + 2 * b + f
                        w = cw[:, tap * 32 + k:tap * 32 + k + 1]
                        src = tp[b][:, f * T:(f + 1) * T - s]
                        dst = conv[:, 2 * b + f, s:T]
                        if tap == 3:
                            ins = nc.vector.tensor_scalar(dst, src, w, cbias[:, k:k + 1], ALU.mult, ALU.add)
                        else:
                            ins = nc.vector.scalar_tensor_tensor(out=dst, in0=src, scalar=w, in1=dst,
                                                                 op0=ALU.mult, op1=ALU.add)
                    if tap:
                        settle(ins)
                ins.then_inc(tp_read[b], 1)

            def gk_read_of(i):
                t, z, c = i // 4, (i // 2) % 2, i % 2
                dve.wait_ge(gk_ready, i + 1)
                if i == 0:
                    dve.wait_ge(masks_ready, 2)
                low = V[:, t, z * GK + c * NC:z * GK + (c + 1) * NC]
                nc.vector.tensor_scalar(low, mx[i % 2][:, :], 0.0, None, ALU.min).then_inc(gk_min, 1)
                dve.wait_ge(gk_min, i + 1)
                nc.vector.scalar_tensor_tensor(out=G[:, t, z, cols(c)], in0=low, scalar=2.0,
                                               in1=mx[i % 2][:, :], op0=ALU.mult, op1=ALU.subtract) \
                    .then_inc(gk_read, 1)

            def gk_decay(i):
                t, z, c = i // 4, (i // 2) % 2, i % 2
                dve.wait_ge(gk_ln, i + 1)
                nc.vector.tensor_tensor(G[:, t, z, cols(c)], V[:, t, z * GK + c * NC:z * GK + (c + 1) * NC],
                                        G[:, t, z, cols(c)], ALU.subtract).then_inc(g_ready, 1)

            def gla_diagonal(h):
                dve.wait_ge(p_ready, score(h, -1) + 1)
                if h == 0:
                    dve.wait_ge(loads["diag"], 16)
                elif h >= 2:
                    dve.wait_ge(tp_ready, 2 * (J["o"].r0 + h - 1))
                nc.vector.tensor_tensor(A_T[:, h % 2, 0:2, :],
                                        mx[1][:, 0:T].rearrange("p (t i) -> p t i", t=2),
                                        diag2[:, :].rearrange("p (t i) -> p t i", t=2), ALU.mult) \
                    .then_inc(a_ready, 1)

            def gla_place(h, i):
                m = score(h, i)
                dve.wait_ge(p_ready, m + 1)
                dve.wait_ge(a_ready, m)
                if i == 0:
                    nc.vector.tensor_copy(A_T[:, h % 2, 2:4, :],
                                          mx[1][:, 0:T].rearrange("p (t i) -> p t i", t=2)).then_inc(a_ready, 1)
                else:
                    nc.vector.copy_predicated(
                        A_T[:, h % 2, 0:2, :].rearrange("p t i -> p (t i)"), masks[:, i - 1, :],
                        mx[1][:, 0:T]).then_inc(a_ready, 1)

            def gla_unit(h, u):
                l, c = half_size(u), u % 2
                n = h * UNITS + u
                dve.wait_ge(ex_ready, n + 1)
                if n >= 4:
                    dve.wait_ge(p_ready, x_free(n))
                for d in range(2):
                    ins = nc.vector.tensor_tensor(
                        halves(X[:, (n // 2) % 2, 0, c:c + 1, :], query_half(d), l),
                        halves(qkT[:, 2 * h + c:2 * h + c + 1, :], query_half(d), l),
                        halves(Ex[:, d:d + 1, :], query_half(d), l), ALU.mult)
                ins.then_inc(xq_ready, 1)
                if u == 0 and h:
                    gla_place(h - 1, SCORES - 1)
                if u == 1:
                    gla_diagonal(h)
                if u >= 2 and u % 2 == 0:
                    gla_place(h, u // 2 - 1)

            def gla_mean(h):
                dve.wait_ge(squared, SQ["gla"] + 2 * (h + 1))
                nc.vector.tensor_scalar(hms[:, 2 * h:2 * h + 2], hss[:, 2 * h:2 * h + 2], 1.0 / GDV, EPS,
                                        ALU.mult, ALU.add).then_inc(ho_ms, 1)

            def gla_normed(h):
                dve.wait_ge(ho_rstd, h + 1)
                for t in range(2):
                    nc.vector.tensor_scalar(H[:, t, cols(h)], tp[t][:, :], hrs[:, 2 * h + t:2 * h + t + 1], None,
                                            ALU.mult).then_inc(tp_read[t], 1)

            def mlstm_weights(h):
                dve.wait_ge(s_ready, h + 1)
                if h:
                    dve.wait_ge(pt_ready, h)
                settle(nc.vector.tensor_scalar(W[:, 0:T], mx[1][:, 0:T], bT[:, 0, h:h + 1], 0.0, ALU.add, ALU.min))
                nc.vector.tensor_scalar(W[:, T:T + P], mx[1][:, P:T], bT[:, 1, h:h + 1], 0.0, ALU.add, ALU.min) \
                    .then_inc(w_ready, 1)

            def mlstm_probs(h):
                dve.wait_ge(wmask_ready, 2 * (h + 1))
                if h:
                    dve.wait_ge(tp_ready, 2 * (J["num"].r0 + h))
                nc.vector.scalar_tensor_tensor(out=PT[:, :], in0=mx[0][:, 0:T + P], scalar=MD ** -0.5,
                                               in1=W[:, :], op0=ALU.mult, op1=ALU.mult).then_inc(pt_ready, 1)

            def mlstm_divide(h):
                r = J["num"].r0 + h
                dve.wait_ge(tp_ready, 2 * r + 2)
                for t in range(2):
                    ins = nc.vector.scalar_tensor_tensor(
                        out=den[:, t:t + 1], in0=tp[t][:, MD:MD + 1], scalar=-1.0, in1=emT[:, t, h:h + 1],
                        op0=ALU.mult, op1=ALU.max)
                settle(ins)
                for t in range(2):
                    ins = nc.vector.tensor_tensor(den[:, t:t + 1], tp[t][:, MD:MD + 1], den[:, t:t + 1], ALU.max)
                settle(ins)
                settle(nc.vector.reciprocal(rden[:, :], den[:, :]))
                for t in range(2):
                    nc.vector.tensor_scalar(VA[:, t, h, 0:MD], tp[t][:, 0:MD], rden[:, t:t + 1], None,
                                            ALU.mult).then_inc(tp_read[t], 1)

            def mlstm_gated(n):
                dve.wait_ge(ho_rstd, GH + 1)
                dve.wait_ge(tp_ready, 2 * (J["ya"].r0 + n))
                for t in range(2):
                    dve.wait_ge(evac[t], E(J["oz"], 2 * n + 1))
                    for h in (2 * n, 2 * n + 1):
                        ins = nc.vector.scalar_tensor_tensor(
                            out=stage[:, t, (h % 2) * MD:(h % 2 + 1) * MD], in0=VA[:, t, h, 0:MD],
                            scalar=hrs[:, 2 * h + t:2 * h + t + 1], in1=GB[:, t, cols(h, MD)],
                            op0=ALU.mult, op1=ALU.mult)
                    ins.then_inc(ya_ready[t], 1)

            def mlstm_forget():
                dve.wait_ge(loads["gbias"], 32)
                for t in range(2):
                    dve.wait_ge(tp_ready, 2 * J["if0"].r0 + t + 1)
                    nc.vector.scalar_tensor_tensor(
                        out=gi[:, t, :], in0=tp[t][:, 0:2 * MH], scalar=rstd[:, S2, t:t + 1],
                        in1=gate_bias[:, :], op0=ALU.mult, op1=ALU.add).then_inc(tp_read[t], 1)
                for t in range(2):
                    dve.wait_ge(tp_read[t], J["if0"].r0 + 1)
                nc.vector.scalar_tensor_tensor(out=minus_abs_f[:, :, :], in0=gi[:, :, MH:2 * MH], scalar=-1.0,
                                               in1=gi[:, :, MH:2 * MH], op0=ALU.mult, op1=ALU.min) \
                    .then_inc(abs_ready, 1)

            def mlstm_log_forget():
                dve.wait_ge(ln_ready, 1)
                nc.vector.scalar_tensor_tensor(out=logf[:, :, :], in0=gi[:, :, MH:2 * MH], scalar=0.0,
                                               in1=lnf[:, :, :], op0=ALU.min, op1=ALU.subtract) \
                    .then_inc(logf_ready, 1)

            def mlstm_scans():
                r = J["if"].r0
                dve.wait_ge(tp_ready, 2 * r + 2)
                dve.wait_ge(ones_set, 2)
                settle(nc.vector.tensor_copy(iR[:, :], tp[0][0:MH, 0:T]))
                nc.vector.tensor_copy(fR[:, :], tp[1][0:MH, 0:T]).then_inc(tp_read[1], 1)
                dve.wait_ge(tp_read[1], r + 1)
                settle(nc.vector.tensor_tensor_scan(Fc[:, :], ones8[:, :], fR[:, :], 0.0, ALU.mult, ALU.add))
                settle(nc.vector.tensor_tensor_scan(mR[:, :], fR[:, :], iR[:, :], 0.0, ALU.add, ALU.max))
                nc.vector.tensor_tensor(bR[:, :], iR[:, :], Fc[:, :], ALU.subtract).then_inc(tp_read[0], 1)
                nc.vector.tensor_tensor(aR[:, :], Fc[:, :], mR[:, :], ALU.subtract).then_inc(scan_ready, 1)

            def mlstm_columns():
                r = J["if"].r0 + 1
                dve.wait_ge(tp_ready, 2 * r + 2)
                nc.vector.tensor_copy(bT[:, :, :], tp[0][:, 0:2 * MH].rearrange("p (t h) -> p t h", t=2)) \
                    .then_inc(tp_read[0], 1)
                nc.vector.tensor_copy(emT[:, :, :], tp[1][:, 0:2 * MH].rearrange("p (t h) -> p t h", t=2)) \
                    .then_inc(tp_read[1], 1)

            def second_norms():
                mean_square(3, SQ["pg"] + 16)
                settle(nc.vector.tensor_reduce(msq[:, 4, :], ssq[:, 4, :, :], AX.X, ALU.add))
                dve.wait_ge(rstd_ready, 4)
                settle(nc.vector.tensor_tensor(msq[:, 4, :], msq[:, 4, :], rstd[:, 3, :], ALU.mult))
                settle(nc.vector.tensor_tensor(msq[:, 4, :], msq[:, 4, :], rstd[:, 3, :], ALU.mult))
                nc.vector.tensor_scalar(msq[:, 4, :], msq[:, 4, :], 1.0 / D, EPS, ALU.mult, ALU.add) \
                    .then_inc(ms_ready, 1)
                dve.wait_ge(rstd_ready, 5)
                nc.vector.tensor_tensor(rstd[:, S2, :], rstd[:, 3, :], rstd[:, 4, :], ALU.mult) \
                    .then_inc(s2_ready, 1)

            def after_split(job, n, j, ns):
                name = job.name
                pj, pn, pns = (job.prev, job.prev.n - 1 if job.prev else 0, job.prev.n - 1 if job.prev else 0) \
                    if ns == 0 else (job, n - 1, ns - 1)
                if name == "qk" and n == 1 and j >= LAG:
                    gk_read_of(j - LAG)
                if name == "qk" and n == 2 and j < LAG:
                    gk_read_of(j - LAG + 8)
                if name == "v" and n == 0:
                    gk_decay(j)
                if hosted(name, n) is not None and j >= LAG:
                    for u in (2 * (j - LAG), 2 * (j - LAG) + 1):
                        gla_unit(hosted(name, n), u)
                if after_head(name, n) is not None:
                    h = after_head(name, n)
                    if j < LAG:
                        for u in (2 * (j - LAG + 8), 2 * (j - LAG + 8) + 1):
                            gla_unit(h, u)
                    if j == LAG and h == GH - 1:
                        gla_place(h, SCORES - 1)
                    if j == LAG + 1:
                        gla_mean(h)
                    if j == LAG + 2:
                        gla_normed(h)
                if name == "oz" and n >= 1 and j == 1:
                    mlstm_divide(n - 1)
                if name == "oz" and j == 4:
                    mlstm_weights(n)
                if name == "oz" and j == 5:
                    mlstm_probs(n)
                if name == "gb" and n == 0 and j == 1:
                    mlstm_divide(MH - 1)
                if pj is not None and j == JE(job):
                    evacuate(pj, pn, pns)
                if pj is not None and pj.name == "pg" and j == 4:
                    dve.wait_ge(sgp_ready, pn + 1)
                    for t in range(2):
                        nc.vector.tensor_tensor(H[:, t, cols(pn)], H[:, t, cols(pn)], gates[:, t, :], ALU.add) \
                            .then_inc(h_ready, 1)
                if pj is not None and pj.name == "pg" and j == 5:
                    dve.wait_ge(loads["fn"], 16)
                    for t in range(2):
                        dve.wait_ge(squared, SQ["pg"] + 4 * pn + t + 1)
                        nc.vector.tensor_tensor(H[:, t, cols(pn)], H[:, t, cols(pn)], fn_bc[:, cols(pn)],
                                                ALU.mult).then_inc(hf_ready[t], 1)
                if name == "f2o" and n == 1 and j == JV(job, "") - 1:
                    xt_low("pt", 0, lambda b: b, None, 1)
                if pj is not None and j == JV(job, pj.name):
                    evacuate_transposed(pj, pn)
                if pj is not None and pj.name == "qk2" and j in (6, 7):
                    convolve(pn, j - 6)
                if name == "qk" and n == 0 and j == 5:
                    dve.wait_ge(rstd_ready, 1)
                    dve.wait_ge(tp_ready, 2 * J["lr0"].r0 + 2)
                    nc.vector.tensor_scalar(stage[:, 1, P:P + 2 * RANK], tp[1][:, 0:2 * RANK], rstd[:, 0, 1:2],
                                            None, ALU.mult).then_inc(tp_read[1], 1)
                if name == "qk" and n == 0 and j == 7:
                    lr_transposed()
                if name == "gb" and n == 0 and j == 4:
                    dve.wait_ge(squared, SQ["mlstm"] + 2 * MH)
                    nc.vector.tensor_scalar(hms[:, :], hss[:, :], 1.0 / MD, EPS, ALU.mult, ALU.add) \
                        .then_inc(ho_ms, 1)
                if name == "gb" and j == 4:
                    mlstm_gated(n)
                if name == "gb" and j == 7:
                    xt_low("ya", n, lambda b: 4 * n + 2 * b, lambda k: vcol("mlstm_norm", k), 2)
                if name == "qk2" and n == 0 and j == 6:
                    mlstm_forget()
                if name == "qk2" and n == 0 and j == 7:
                    mlstm_log_forget()
                if name == "qk2" and n == 1 and j == 3:
                    mlstm_scans()
                if name == "qk2" and n == 1 and j == 5:
                    mlstm_columns()
                if name == "f1" and ns == 0 and j == 4:
                    mean_square(1, SQ["wo"] + 8)
                if name == "pp" and n == 1:
                    mean_square(2, SQ["f2o"] + 8)
                if name == "ub" and n == 0 and j == 7:
                    second_norms()

            dve.wait_ge(tp_ready, 2)
            nc.vector.tensor_copy(vec[:, :], tp[1][:, 0:VEC_ROWS]).then_inc(tp_read[1], 1)
            settle(nc.vector.tensor_copy(cbias[:, :], tp[0][:, P:P + 32]))
            nc.vector.tensor_copy(cw[:, :], tp[0][:, 0:P]).then_inc(tp_read[0], 1)
            dve.wait_ge(tp_read[1], 1)
            for j in range(HL_SLOTS):
                split_lo(J["lr"], 0, j, 0)
            for r in range(4):
                xt_low("x", r, lambda b: 4 * r + 2 * b, lambda k: vcol("mixer_norm", k), 2)
            mean_square(0, SQ["x"] + 8)

            for job in JOBS:
                def column_tile(n, ns):
                    for j in range(job.G):
                        if not (job.name == "lr" and j < HL_SLOTS):
                            split_lo(job, n, j, ns)
                        after_split(job, n, j, ns)
                if job.name in LOOPED:
                    column_tile(0, 0)
                    with dve.Fori(0, loop_passes(job)) as i:
                        for b in (1, 2):
                            column_tile(2 * i + b, b)
                    column_tile(job.n - 1, job.n - 1)
                else:
                    for n in range(job.n):
                        column_tile(n, n)
            evacuate(J["out"], 3, 3)
            mean_square(5, SQ["out"] + 8)
            dve.wait_ge(rstd_ready, 6)
            dve.wait_ge(x2_ready, 2)
            for n in range(4):
                for t in range(2):
                    dve.wait_ge(evac[t], E(J["out"], n))
                    nc.vector.scalar_tensor_tensor(
                        out=OUT[:, t, cols(n)], in0=OUT[:, t, cols(n)], scalar=rstd[:, 5, t:t + 1],
                        in1=H[:, t, cols(n)], op0=ALU.mult, op1=ALU.add).then_inc(y_ready, 1)


def constants():
    import numpy as np

    s, r = np.arange(P)[:, None], np.arange(P)[None, :]
    sums = np.zeros((P, 18, P), np.float32)
    masks = np.zeros((P, 7, P), np.float32)
    for d in range(2):
        if d == 0:
            sums[:, 0] = s > r
            sums[:, 1] = s <= r
        else:
            sums[:, 9] = s >= r
            sums[:, 10] = s < r
        for i, l in enumerate(LEVELS):
            same = s // (2 * l) == r // (2 * l)
            s_up, r_up = (s // l) % 2 == 1, (r // l) % 2 == 1
            if d == 0:
                keep = (r_up & s_up & (s <= r)) | (~r_up & ~s_up & (s > r))
                pair = same & ~s_up & r_up
            else:
                keep = (~r_up & ~s_up & (s >= r)) | (r_up & s_up & (s < r))
                pair = same & s_up & ~r_up
            sums[:, 9 * d + 2 + i] = keep & same
            masks[:, i, :] += pair
    diag = np.tile(2.0 * np.eye(P, dtype=np.float32), (1, 2))
    t = np.arange(T)
    windows = np.zeros((T, 4, T), np.float64)
    for g, w in enumerate(POOL_WINDOWS):
        low = np.maximum(t + 1 - w, 0)
        inside = (t[:, None] >= low[None, :]) & (t[:, None] <= t[None, :])
        windows[:, g] = inside / (t + 1 - low)[None, :] - np.eye(T)
    packed = np.concatenate([windows[0:P], windows[P:T, :, P:T]], axis=2)
    return {
        "c_ident": np.eye(P, dtype=np.float32), "c_sums": sums.reshape(P, -1),
        "c_masks": masks.reshape(P, -1), "c_diag": diag,
        "c_windows": packed.reshape(P, -1).astype(np.float32),
    }


_INS = ["x", "p", "mixer_norm", "gla_w_in", "gla_w_gate_up", "gla_b_gate", "gla_out_norm", "gla_w_out",
        "ffn_norm", "ffn_w_in", "ffn_w_out", "ple_norm", "ple_w_gate", "ple_w_proj", "final_norm",
        "norm_pre_w_2", "w_in_2", "mlstm_i_bias_2", "mlstm_f_bias_2", "qk_conv_w_2", "qk_conv_b_2",
        "mlstm_norm_w_2", "pool_w_2", "pool_scale_2", "w_proj_mlstm_2", "w_proj_pool_2", "w_out_2",
        "norm_post_w_2"]
_MATRICES = ("gla_w_in", "gla_w_out", "ffn_w_in", "ffn_w_out", "ple_w_gate", "ple_w_proj", "w_in_2",
             "w_proj_mlstm_2", "w_proj_pool_2", "w_out_2")


def kernel(**inputs):
    import numpy as np
    import concourse.bacc as bacc
    from concourse.bass_utils import run_bass_kernel_spmd

    nc = bacc.Bacc("TRN2", target_bir_lowering=False, num_devices=1)
    arrays, args = {}, []
    for name in _INS:
        a = np.ascontiguousarray(inputs[name])
        if name in _MATRICES:
            a = a.reshape(a.shape[1:])
        arrays["in_" + name] = a
    for name, a in constants().items():
        arrays["in_" + name] = a
    for name, a in arrays.items():
        args.append(nc.dram_tensor(name, a.shape, mybir.dt.from_np(a.dtype), kind="ExternalInput").ap())
    args.append(nc.dram_tensor("out_y", (1, T, D), F32, kind="ExternalOutput").ap())
    build(nc, *args)
    r = run_bass_kernel_spmd(nc, [arrays], core_ids=[0])
    return r.results[0]["out_y"]
```
